# Optimizing a Trainium2 kernel written in Bass

```python
import jax, jax.numpy as jnp
from jax import lax
import numpy as np

D_MODEL = 2048
BATCH = 1
SEQ = 256
DEPTH = 2

CHUNK = 64
EPS = 1e-6
A_WIDTH = D_MODEL // 2
A_CONV = 31
B_HEADS = 8
B_DK = 128
B_DV = (D_MODEL - A_WIDTH) // B_HEADS
B_WIDTH = B_HEADS * B_DV
EVEN_IN = 2 * A_WIDTH + 3 * B_HEADS * B_DK + B_WIDTH
C_WIDTH = D_MODEL // 2
C_CONV = 3
D_HEAD_DIM = 64
D_Q_HEADS = (D_MODEL - C_WIDTH) // D_HEAD_DIM
D_KV_HEADS = D_Q_HEADS // 8
D_GROUP = D_Q_HEADS // D_KV_HEADS
WINDOW = 128
WINDOW_CHUNKS = WINDOW // CHUNK
ODD_IN = 3 * C_WIDTH + D_Q_HEADS * D_HEAD_DIM + 2 * D_KV_HEADS * D_HEAD_DIM
D_FF = 4 * D_MODEL
N_EVEN = (DEPTH + 1) // 2
N_ODD = DEPTH // 2

kernel_name = "hybrid_conformer_hgrn2_shortconv_swa_sink"

def rmsnorm(x, w):
    xf = x.astype(jnp.float32)
    y = xf * lax.rsqrt(jnp.mean(xf * xf, axis=-1, keepdims=True) + EPS)
    return (y * w.astype(jnp.float32)).astype(x.dtype)

def layernorm(x, w, b):
    xf = x.astype(jnp.float32)
    mu = jnp.mean(xf, axis=-1, keepdims=True)
    var = jnp.mean(jnp.square(xf - mu), axis=-1, keepdims=True)
    y = (xf - mu) * lax.rsqrt(var + EPS)
    return (y * w.astype(jnp.float32) + b.astype(jnp.float32)).astype(x.dtype)

def causal_dwconv(x, w):
    K, C = w.shape
    return lax.conv_general_dilated(
        x, w[:, None, :].astype(x.dtype), window_strides=(1,), padding=[(K - 1, 0)],
        dimension_numbers=("NWC", "WIO", "NWC"), feature_group_count=C)

def conformer_conv(u_val, u_gate, dw_w, dw_b, ln_w, ln_b):
    h = u_val * jax.nn.sigmoid(u_gate)
    h = causal_dwconv(h, dw_w) + dw_b.astype(h.dtype)
    h = layernorm(h, ln_w, ln_b)
    return jax.nn.silu(h)

def hgrn2_chunk_step(state, inp):
    q, logf, k, v = inp
    L = q.shape[2]
    b = jnp.cumsum(logf, axis=2)
    tri = jnp.tril(jnp.ones((L, L), dtype=bool))
    diff = b[:, :, :, None, :] - b[:, :, None, :, :]
    decay = jnp.exp(jnp.where(tri[None, None, :, :, None], diff, -jnp.inf))
    attn = jnp.einsum("bhtk,bhtsk,bhsk->bhts", q, decay, k)
    o = jnp.einsum("bhts,bhsv->bhtv", attn, v)
    o = o + jnp.einsum("bhtk,bhkv->bhtv", q * jnp.exp(b), state)
    b_last = b[:, :, -1:, :]
    new_state = state * jnp.exp(b_last[:, :, 0, :, None]) + jnp.einsum(
        "bhsk,bhsv->bhkv", k * jnp.exp(b_last - b), v)
    return new_state, o

def hgrn2(q, f_logit, i_val, g, lb, norm_w):
    Bsz, S, _ = q.shape
    nC = S // CHUNK
    f = lb + (1.0 - lb) * jax.nn.sigmoid(f_logit.astype(jnp.float32))
    logf = jnp.log(f)
    k = 1.0 - f

    def heads(t, d):
        return t.astype(jnp.float32).reshape(Bsz, nC, CHUNK, B_HEADS, d).transpose(1, 0, 3, 2, 4)

    s0 = jnp.zeros((Bsz, B_HEADS, B_DK, B_DV), jnp.float32)
    _, o = lax.scan(hgrn2_chunk_step, s0,
                    (heads(q, B_DK), heads(logf, B_DK), heads(k, B_DK), heads(i_val, B_DV)))
    o = o.transpose(1, 0, 3, 2, 4).reshape(Bsz, S, B_HEADS, B_DV)
    o = rmsnorm(o, norm_w).reshape(Bsz, S, B_WIDTH)
    return o.astype(q.dtype) * jax.nn.silu(g)

def short_gated_conv(h, gate_b, gate_c, conv_w):
    return gate_b * causal_dwconv(gate_c * h, conv_w)

def swa_sink_attention(q, k, v, sinks):
    Bsz, S, _ = q.shape
    L, W = CHUNK, WINDOW_CHUNKS
    nC = S // L
    qb = q.reshape(Bsz, nC, L, D_KV_HEADS, D_GROUP, D_HEAD_DIM) * (D_HEAD_DIM ** -0.5)

    def band(t):
        tc = t.reshape(Bsz, nC, L, D_KV_HEADS, D_HEAD_DIM)
        tp = jnp.pad(tc, ((0, 0), (W - 1, 0), (0, 0), (0, 0), (0, 0)))
        return jnp.concatenate([tp[:, w:w + nC] for w in range(W)], axis=2)

    kb, vb = band(k), band(v)
    s = jnp.einsum("bcikgd,bcjkd->bckgij", qb, kb).astype(jnp.float32)
    slopes = 2.0 ** (-8.0 * jnp.arange(1, D_Q_HEADS + 1, dtype=jnp.float32) / D_Q_HEADS)
    dist = jnp.abs(jnp.arange(L)[:, None] + (W - 1) * L - jnp.arange(W * L)[None, :]).astype(jnp.float32)
    bias = (-slopes[:, None, None] * dist).reshape(D_KV_HEADS, D_GROUP, L, W * L)
    s = s + bias[None, None]
    valid = (jnp.arange(nC)[:, None] * L + jnp.arange(W * L)[None, :]) >= (W - 1) * L
    s = jnp.where(valid[None, :, None, None, None, :], s, -jnp.inf)
    sink = jnp.broadcast_to(sinks.astype(jnp.float32).reshape(D_KV_HEADS, D_GROUP, 1, 1),
                            s.shape[:-1] + (1,))
    p = jax.nn.softmax(jnp.concatenate([s, sink], axis=-1), axis=-1)[..., :-1]
    o = jnp.einsum("bckgij,bcjkd->bcikgd", p.astype(v.dtype), vb)
    return o.reshape(Bsz, S, D_Q_HEADS * D_HEAD_DIM)

def setup_inputs(seed: int = 0) -> dict:
    key = jax.random.key(seed)
    ks = jax.random.split(key, 24)
    f32 = jnp.float32
    nrm = lambda k, shape, scale: jax.random.normal(k, shape, f32) * scale
    gain = lambda k, shape: 1.0 + 0.02 * jax.random.normal(k, shape, f32)
    return {
        "x": jax.random.normal(ks[0], (BATCH, SEQ, D_MODEL), f32),
        "w_in_even": nrm(ks[1], (N_EVEN, D_MODEL, EVEN_IN), D_MODEL ** -0.5),
        "w_out_even": nrm(ks[2], (N_EVEN, A_WIDTH + B_WIDTH, D_MODEL), (A_WIDTH + B_WIDTH) ** -0.5),
        "a_dw_w": nrm(ks[3], (N_EVEN, A_CONV, A_WIDTH), A_CONV ** -0.5),
        "a_dw_b": nrm(ks[4], (N_EVEN, A_WIDTH), 0.02),
        "a_ln_w": gain(ks[5], (N_EVEN, A_WIDTH)),
        "a_ln_b": nrm(ks[6], (N_EVEN, A_WIDTH), 0.02),
        "b_lb_logits": nrm(ks[7], (N_EVEN + 1, B_HEADS * B_DK), 0.5),
        "b_norm_w": gain(ks[8], (N_EVEN, B_DV)),
        "w_in_odd": nrm(ks[9], (N_ODD, D_MODEL, ODD_IN), D_MODEL ** -0.5),
        "w_out_odd": nrm(ks[10], (N_ODD, C_WIDTH + D_Q_HEADS * D_HEAD_DIM, D_MODEL),
                          (C_WIDTH + D_Q_HEADS * D_HEAD_DIM) ** -0.5),
        "c_conv_w": nrm(ks[11], (N_ODD, C_CONV, C_WIDTH), C_CONV ** -0.5),
        "d_sinks": nrm(ks[12], (N_ODD, D_Q_HEADS), 0.5),
        "norm_pre_mix": gain(ks[13], (DEPTH, D_MODEL)),
        "norm_post_mix": gain(ks[14], (DEPTH, D_MODEL)),
        "norm_pre_ffn": gain(ks[15], (DEPTH, D_MODEL)),
        "norm_post_ffn": gain(ks[16], (DEPTH, D_MODEL)),
        "w_ffn_up": nrm(ks[17], (DEPTH, D_MODEL, D_FF), D_MODEL ** -0.5),
        "w_ffn_down": nrm(ks[18], (DEPTH, D_FF, D_MODEL), D_FF ** -0.5),
    }

def reference(x, w_in_even, w_out_even, a_dw_w, a_dw_b, a_ln_w, a_ln_b, b_lb_logits, b_norm_w,
              w_in_odd, w_out_odd, c_conv_w, d_sinks, norm_pre_mix, norm_post_mix,
              norm_pre_ffn, norm_post_ffn, w_ffn_up, w_ffn_down):
    lb_all = jnp.cumsum(jax.nn.softmax(b_lb_logits.astype(jnp.float32), axis=0), axis=0)
    for l in range(DEPTH):
        j = l // 2
        h = rmsnorm(x, norm_pre_mix[l])
        if l % 2 == 0:
            u = h @ w_in_even[j]
            a_val, a_gate, b_q, b_f, b_i, b_g = jnp.split(
                u, np.cumsum([A_WIDTH, A_WIDTH, B_HEADS * B_DK, B_HEADS * B_DK, B_WIDTH]), axis=-1)
            a_out = conformer_conv(a_val, a_gate, a_dw_w[j], a_dw_b[j], a_ln_w[j], a_ln_b[j])
            b_out = hgrn2(b_q, b_f, b_i, b_g, lb_all[j], b_norm_w[j])
            y = jnp.concatenate([a_out, b_out], axis=-1) @ w_out_even[j]
        else:
            u = h @ w_in_odd[j]
            c_h, c_b, c_c, d_q, d_k, d_v = jnp.split(
                u, np.cumsum([C_WIDTH, C_WIDTH, C_WIDTH, D_Q_HEADS * D_HEAD_DIM,
                              D_KV_HEADS * D_HEAD_DIM]), axis=-1)
            c_out = short_gated_conv(c_h, c_b, c_c, c_conv_w[j])
            d_out = swa_sink_attention(d_q, d_k, d_v, d_sinks[j])
            y = jnp.concatenate([c_out, d_out], axis=-1) @ w_out_odd[j]
        x = x + rmsnorm(y, norm_post_mix[l])
        h = rmsnorm(x, norm_pre_ffn[l])
        y = jnp.square(jax.nn.relu(h @ w_ffn_up[l])) @ w_ffn_down[l]
        x = x + rmsnorm(y, norm_post_ffn[l])
    return x


_drawn_inputs = setup_inputs


def setup_inputs(seed=0):
    import zlib

    import numpy as np

    out = dict(_drawn_inputs(seed))
    spreads = {}
    factors = {'a_ln_w': 42.85,
     'a_ln_b': 43.061,
     'b_norm_w': 51.467,
     'd_sinks': 6.194,
     'norm_pre_ffn': 2.904,
     'norm_post_ffn': 9.028,
     'norm_post_mix': 2.892}
    for name, (base, spread) in spreads.items():
        noise = np.random.default_rng([zlib.crc32(name.encode()), seed]).standard_normal(out[name].shape)
        drawn = base * np.exp(spread * noise) if base else spread * noise
        out[name] = __import__('jax').numpy.asarray(drawn.astype(out[name].dtype))
    for name, factor in factors.items():
        out[name] = (out[name] * factor).astype(out[name].dtype)
    return out
```

```python
from contextlib import ExitStack

import numpy as np

import concourse.bass as bass
from concourse import mybir

F32 = mybir.dt.float32
F32R = mybir.dt.float32r
ALU = mybir.AluOpType
ACT = mybir.ActivationFunctionType
AX_X = mybir.AxisListType.X

P = 128
SEQ = 256
D = 2048
KT = D // P
FF = 4 * D
COLS = 256
MT = COLS // P
PIECES = 4
KP = KT // PIECES
PW = KP * COLS
EPS = 1e-6

A_TILES = 8
A_CONV = 31
HEADS = 8
CHUNK = 64
C_TILES = 8
C_CONV = 3
Q_HEADS, GROUPS, DH = 16, 2, 64
WIN = 128

IN0 = [x for j in range(4) for x in (("a", j), ("f", j))] + \
      [x for j in range(4) for x in (("a", 4 + j), ("i", j))] + \
      [("q", j) for j in range(4)] + [("g", j) for j in range(4)]
IN1 = [("kv", 0)] + [("q", j) for j in range(4)] + [("c", j) for j in range(12)]
OUT_TASKS = D // COLS
BLOCK = D // COLS
FF_BLOCKS = FF // D
START_IN0 = 0
START_OUT0 = START_IN0 + len(IN0)
START_FF0 = START_OUT0 + OUT_TASKS
START_IN1 = START_FF0 + 2 * BLOCK * FF_BLOCKS
START_OUT1 = START_IN1 + len(IN1)
START_FF1 = START_OUT1 + OUT_TASKS
TASKS = START_FF1 + 2 * BLOCK * FF_BLOCKS

V_NORM = 0
V_DW = V_NORM + 8 * KT
V_DWB = V_DW + A_TILES * A_CONV
V_LNW = V_DWB + A_TILES
V_LNB = V_LNW + A_TILES
V_LB = V_LNB + A_TILES
V_BN = V_LB + 2 * HEADS
V_CC = V_BN + 1
V_SINK = V_CC + C_TILES * C_CONV
V_N = V_SINK + Q_HEADS // 2

SCAN_STEP = 8
LN_STEP = 19
ATT_STEP = 5

LEVELS = 8
C_ID = 0
C_ONE = C_ID + P
C_MASK = C_ONE + P
C_RESET = C_MASK + LEVELS * P
C_N = C_RESET + SEQ
HALVES = [0, 1, 2, 4, 8, 16, 32, 64]


class Clock:

    def __init__(self, eng, sem):
        self.eng, self.sem, self.n, self.rt = eng, sem, 0, 0

    def mark(self, ins):
        self.n += 1
        ins.then_inc(self.sem, 1)

    def settle(self, back=0):
        if self.n > back:
            self.eng.wait_ge(self.sem, self.rt + (self.n - back))

    def link(self, ins):
        self.mark(ins)
        self.settle()


def bass_hybrid_trunk(nc: bass.Bass, w, xin, vecs, consts, bias, xsave, out):
    with ExitStack() as ctx:
        def sb(name, cols, dt=F32):
            return ctx.enter_context(nc.sbuf_tensor(name, [P, cols], dt))

        def sem(name):
            return ctx.enter_context(nc.semaphore(name))

        raw = sb("raw", PIECES * PW)
        w_hi = sb("w_hi", 2 * PIECES * PW, F32R)
        w_lo = sb("w_lo", 2 * PIECES * PW, F32R)
        in_hi = sb("in_hi", KT * SEQ, F32R)
        in_lo = sb("in_lo", KT * SEQ, F32R)
        mid_hi = sb("mid_hi", KT * SEQ, F32R)
        mid_lo = sb("mid_lo", KT * SEQ, F32R)
        x = sb("x", KT * SEQ)
        y = sb("y", KT * SEQ)
        vec = sb("vec", V_N)
        con = sb("con", C_N)
        rpre = sb("rpre", SEQ)
        rpost = sb("rpost", SEQ)
        sqsum = sb("sqsum", SEQ)
        u = sb("u", MT * SEQ)
        g = sb("g", MT * SEQ)
        wk = sb("wk", 3072)
        hpad = sb("hpad", 2 * (SEQ + A_CONV - 1))
        acc2 = sb("acc2", SEQ)
        pairs = sb("pairs", 3 * P)
        small = sb("small", 64)

        bank = [ctx.enter_context(nc.psum_tensor(f"bank{n}", [P, 512], F32)) for n in range(8)]
        dense_bank, stat, lev, misc = bank[0:4], bank[4], [bank[5], bank[7]], bank[6]

        ident = con[:, C_ID:C_ID + P]
        ones = con[:, C_ONE:C_ONE + P]
        eps = small[:, 0:1]
        lb, omlb = small[:, 8:16], small[:, 16:24]
        tail2 = small[:, 24:32]
        mx, esink, den, rden = small[:, 32:36], small[:, 36:40], small[:, 40:44], small[:, 44:48]

        conv, kk = x[:, 0:2048], x[:, 2048:4096]
        bb, qq = y[:, 0:2048], y[:, 2048:4096]
        vtok, mm = wk[:, 0:2048], wk[:, 2048:3072]
        kT, vT, vwin = x[:, 0:256], x[:, 256:512], x[:, 512:896]
        sc, pT = x[:, 896:1408], x[:, 1408:1920]
        cbuf, cpad, cacc = x[:, 1920:3456], x[:, 3456:3456 + SEQ + 2], x[:, 3714:3970]
        qT, dT = y[:, 0:2048], y[:, 2048:4096]

        def v3(ap, c):
            return ap.rearrange("p (a b) -> p a b", b=c)

        def per_token(ap, n):
            return ap.unsqueeze(1).to_broadcast([P, n, SEQ])

        def tile(ap, k, n=1):
            return ap[:, k * SEQ:(k + n) * SEQ]

        def vcol(c):
            return vec[:, c:c + 1]

        s_vec, s_con, s_bias = sem("vectors_landed"), sem("constants_landed"), sem("bias_landed")
        s_x, s_back, s_spill, s_out = sem("x_landed"), sem("x_back"), sem("x_spilled"), sem("out_written")
        s_raw = [sem(f"piece{n}_landed") for n in range(PIECES)]
        s_hi, s_lo, s_mul = sem("weights_high"), sem("weights_split"), sem("pieces_multiplied")
        s_taken = sem("results_taken")
        s_pool = sem("pool_clock")
        s_act, s_dve = sem("act_clock"), sem("dve_clock")
        s_xn, s_inh, s_inl = sem("x_updated"), sem("input_high"), sem("input_split")
        s_xsq, s_sum, s_stat, s_rpre, s_rpost = (sem("x_squared"), sem("squares_added"), sem("sums_of_squares"),
                                                 sem("rms_pre"), sem("rms_post"))
        s_sqf = sem("square_buffer_added")
        s_yr = sem("y_normed")
        s_g, s_mid = sem("g_made"), sem("mid_split")
        s_eps, s_lbx, s_lbe = sem("eps_set"), sem("bound_logits_shifted"), sem("bound_exp")
        s_f, s_lnf, s_scan = sem("forget_gates"), sem("forget_logs"), sem("decays_summed")
        s_vt, s_gate, s_gate_hi = sem("v_transposed"), sem("gated"), sem("gated_high")
        s_conv, s_lnsum, s_cent = sem("convolved"), sem("channel_sum"), sem("centred")
        s_csq, s_lnsq, s_lnr, s_lnn = sem("centred_squared"), sem("squares_summed"), sem("inverse_deviation"), sem("normed")
        s_lna, s_lns, s_lnh = sem("affine_sigmoid"), sem("swish"), sem("swish_high")
        s_dist, s_dec, s_kq, s_lv = sem("exponents"), sem("decays"), sem("decayed_kq"), sem("level_products")
        s_xdec, s_xp, s_pairs = sem("cross_decays"), sem("cross_product"), sem("pair_weights")
        s_o, s_oc, s_osq, s_on, s_or = (sem("head_output"), sem("head_output_copied"), sem("head_squared"),
                                        sem("head_square_sum"), sem("head_inverse_rms"))
        s_win, s_sc, s_sm, s_ex, s_p = sem("v_windows"), sem("scores"), sem("scores_shifted"), sem("exponentials"), sem("probabilities")
        s_pt, s_ptc, s_pv, s_d = sem("probabilities_transposed"), sem("probabilities_copied"), sem("weighted_v"), sem("attended")
        s_dhi, s_dlo = sem("attended_high"), sem("attended_split")
        s_c, s_chi = sem("short_convolved"), sem("short_convolved_high")

        block = ctx.enter_context(nc.Block())

        G0 = {}
        for i, (kind, j) in enumerate(IN0):
            if kind in "afg":
                G0[i] = len(G0) + 1
        N_G0 = len(G0)

        G_OUT0 = N_G0
        G_FF0 = G_OUT0 + OUT_TASKS
        G_OUT1 = G_FF0 + BLOCK * FF_BLOCKS + BLOCK
        G_FF1 = G_OUT1 + OUT_TASKS
        M_OUT0 = 0
        M_FF0 = M_OUT0 + KT // 2
        M_OUT1 = M_FF0 + BLOCK * FF_BLOCKS
        M_FF1 = M_OUT1 + C_TILES // 2

        def wait(eng, s, n, blk=0, per=0):
            eng.wait_ge(s, blk * per + n if per else n)

        @block.sync
        def _(sp):
            sp.dma_start(vec[:, :], vecs).then_inc(s_vec, 16)
            sp.dma_start(x[:, :], xin).then_inc(s_x, 16)

            def piece(i, pc, first=False, reg=False):
                if not first:
                    sp.wait_ge(s_lo, i * PIECES + (pc + 1 - PIECES))
                src = w[i, :, pc * PW:(pc + 1) * PW] if not reg else w[bass.ds(i, 1), :, pc * PW:(pc + 1) * PW].rearrange("a p n -> (a p) n")
                sp.dma_start(raw[:, pc * PW:(pc + 1) * PW], src).then_inc(s_raw[pc], 16)

            for pc in range(PIECES):
                piece(0, pc, first=True)
            sp.dma_start(con[:, :], consts).then_inc(s_con, 16)

            with sp.Fori(1, TASKS) as i:
                for pc in range(PIECES):
                    piece(i, pc, reg=True)
            for k in range(0, KT, 4):
                sp.wait_ge(s_xn, 3 * KT + k + 4)
                sp.dma_start(out[:, k * SEQ:(k + 4) * SEQ], tile(x, k, 4)).then_inc(s_out, 16)
            sp.wait_ge(s_out, 64)

        @block.gpsimd
        def _(pool):
            def norm(n):
                pool.wait_ge(s_rpost, n)
                for k in range(KT):
                    pool.tensor_tensor(tile(y, k), tile(y, k), rpost[:, :], ALU.mult).then_inc(s_yr, 1)

            pool.wait_ge(s_mid, M_OUT0 + KT // 2)
            pool.dma_start(x[:, :], xin).then_inc(s_back, 16)
            norm(1)
            norm(2)
            pool.wait_ge(s_xsq, 3)
            pool.dma_start(xsave, x[:, :]).then_inc(s_spill, 16)
            pool.dma_start(wk[:, 0:1024], bias).then_inc(s_bias, 16)
            pool.wait_ge(s_mid, M_OUT1 + C_TILES // 2)
            pool.wait_ge(s_dlo, 1)
            pool.wait_ge(s_spill, 16)
            pool.dma_start(x[:, :], xsave).then_inc(s_back, 16)
            norm(3)
            norm(4)

        @block.tensor
        def _(pe):
            pe.wait_ge(s_con, 16)

            def dense(i, blk=0, per=0, moving=(in_hi, in_lo), ready=None):
                mh, ml = moving
                for pc in range(PIECES):
                    wait(pe, s_lo, i * PIECES + pc + 1, blk, per * PIECES)
                    if pc == 0 and i >= 4:
                        wait(pe, s_taken, i - 3, blk, per)
                    for kq in range(KP):
                        k = pc * KP + kq
                        if ready:
                            ready(k)
                        for m in range(MT):
                            o = ((i % 2) * PIECES + pc) * PW + kq * COLS + m * P
                            dst = dense_bank[i % 4][:, m * SEQ:(m + 1) * SEQ]
                            wh, wl = w_hi[:, o:o + P], w_lo[:, o:o + P]
                            xh, xl = tile(mh, k), tile(ml, k)
                            pe.matmul(dst, wh, xh, start=(k == 0 and m == 0), stop=False, skip_group_check=True)
                            pe.matmul(dst, wh, xl, start=False, stop=False, skip_group_check=True)
                            mmul = pe.matmul(dst, wl, xh, start=False, stop=(k == KT - 1), skip_group_check=True)
                    mmul.then_inc(s_mul, 1)

            def in_ready(phase):
                return lambda k: pe.wait_ge(s_inl, phase * KT + k + 1)

            def norm_sum(n):
                pe.wait_ge(s_sum, n)
                pe.matmul(stat[:, 0:SEQ], ones, sqsum[:, :], start=True, stop=True).then_inc(s_stat, 1)

            def hgrn(n):
                for grp in range(2):
                    pe.wait_ge(s_kq, 3 * n + grp + 1)
                    for tt in range(2):
                        for l in range(4):
                            if grp == 0 and l == 0:
                                a, b = tile(kk, n)[:, tt * P:(tt + 1) * P], tile(qq, n)[:, tt * P:(tt + 1) * P]
                            else:
                                m0 = (l - 1 if grp == 0 else l) * SEQ + tt * P
                                a = b = mm[:, m0:m0 + P]
                            ins = pe.matmul(lev[tt][:, l * P:(l + 1) * P], a, b, start=(l == 0), stop=True,
                                            skip_group_check=True)
                        ins.then_inc(s_lv, 1)
                pe.wait_ge(s_kq, 3 * n + 3)
                pe.matmul(misc[:, 2 * P:3 * P], mm[:, 0:P], mm[:, P:2 * P], start=True, stop=True).then_inc(s_xp, 1)
                pe.wait_ge(s_pairs, n + 1)
                v0, v1 = vtok[:, n * P:(n + 1) * P], vtok[:, (HEADS + n) * P:(HEADS + n + 1) * P]
                pe.matmul(misc[:, 0:P], v0, pairs[:, 0:P], start=True, stop=True, skip_group_check=True)
                pe.matmul(misc[:, P:2 * P], v0, pairs[:, 2 * P:3 * P], start=False, stop=False, skip_group_check=True)
                pe.matmul(misc[:, P:2 * P], v1, pairs[:, P:2 * P], start=False, stop=True,
                          skip_group_check=True).then_inc(s_o, 1)
                pe.wait_ge(s_osq, n + 1)
                pe.matmul(stat[:, 0:SEQ], ones, g[:, 0:SEQ], start=True, stop=True).then_inc(s_on, 1)

            def layernorm():
                pe.wait_ge(s_conv, 1)
                for j in range(A_TILES):
                    ins = pe.matmul(stat[:, 0:SEQ], ones, tile(conv, j), start=(j == 0), stop=(j == A_TILES - 1))
                ins.then_inc(s_lnsum, 1)
                for h in range(2):
                    pe.wait_ge(s_csq, h + 1)
                    for q in range(4):
                        ins = pe.matmul(stat[:, SEQ:2 * SEQ], ones, tile(mm, q),
                                        start=(h == 0 and q == 0), stop=(h == 1 and q == 3))
                    ins.then_inc(s_lnsq, 1)

            def attention(r):
                c, gr = r // GROUPS, r % GROUPS
                n = CHUNK if c == 0 else WIN
                t0 = max(c - 1, 0) * CHUNK
                rows = slice(gr * DH, (gr + 1) * DH)
                for jp in range(4):
                    q0 = (c * C_TILES + 2 * jp) * CHUNK
                    q2 = qT[rows, q0:q0 + 2 * CHUNK]
                    ins = pe.matmul(lev[0][:, jp * P:jp * P + n], q2, kT[rows, t0:t0 + n],
                                    start=(jp == 0), stop=True, skip_group_check=True)
                ins.then_inc(s_sc, 1)
                pe.wait_ge(s_p, r + 1)
                for jp in range(4):
                    ins = pe.transpose(lev[1][0:n, jp * P:(jp + 1) * P], sc[:, jp * P:jp * P + n], ident)
                ins.then_inc(s_pt, 1)
                pe.wait_ge(s_ptc, r + 1)
                v0 = max(c - 1, 0) * P + gr * DH
                pe.matmul(misc[rows, :], vwin[0:n, v0:v0 + DH], pT[0:n, :], start=True, stop=True).then_inc(s_pv, 1)
                pe.wait_ge(s_d, r + 1)

            dense(0, ready=in_ready(0))
            norm_sum(1)
            for t in range(1, len(IN0)):
                dense(t)
                kind, j = IN0[t - 1]
                if kind == "i":
                    pe.wait_ge(s_taken, t)
                    for m in range(MT):
                        for tt in range(2):
                            ins = pe.transpose(misc[:, (2 * m + tt) * P:(2 * m + tt + 1) * P],
                                               tile(qq, 2 * j + m)[:, tt * P:(tt + 1) * P], ident)
                    ins.then_inc(s_vt, 1)
                if IN0[t][0] == "q":
                    hgrn(2 * IN0[t][1])
                    hgrn(2 * IN0[t][1] + 1)
                if t == LN_STEP:
                    layernorm()

            def mid_ready(base, blk=0, per=0):
                return lambda k: wait(pe, s_mid, base + k // 2 + 1, blk, per) if k % 2 == 0 else None

            def mid_ready1(k):
                if k < C_TILES:
                    pe.wait_ge(s_mid, M_OUT1 + k // 2 + 1)
                elif k == C_TILES:
                    pe.wait_ge(s_dlo, 1)

            def out_projection(start, ready, n):
                for t in range(OUT_TASKS):
                    dense(start + t, moving=(mid_hi, mid_lo), ready=ready if t == 0 else None)
                norm_sum(n)

            def ffn(start, base, phase, n):
                dense(start, ready=in_ready(phase))
                norm_sum(n)
                for t in range(1, BLOCK):
                    dense(start + t)
                for t in range(BLOCK):
                    dense(start + BLOCK + t, moving=(mid_hi, mid_lo), ready=mid_ready(base) if t == 0 else None)
                with pe.Fori(1, FF_BLOCKS) as blk:
                    for t in range(BLOCK):
                        dense(start + t, blk, 2 * BLOCK)
                    for t in range(BLOCK):
                        dense(start + BLOCK + t, blk, 2 * BLOCK, moving=(mid_hi, mid_lo),
                              ready=mid_ready(base, blk, BLOCK) if t == 0 else None)
                norm_sum(n + 1)

            out_projection(START_OUT0, mid_ready(M_OUT0), 2)
            ffn(START_FF0, M_FF0, 1, 3)

            dense(START_IN1, ready=in_ready(2))
            norm_sum(5)
            for t in range(1, len(IN1)):
                dense(START_IN1 + t)
                if t == 1:
                    pe.wait_ge(s_taken, START_IN1 + 1)
                    for c in range(1, 4):
                        ins = pe.transpose(misc[:, (c - 1) * P:c * P], vT[:, (c - 1) * CHUNK:(c + 1) * CHUNK], ident)
                    ins.then_inc(s_win, 1)
                if t == ATT_STEP:
                    pe.wait_ge(s_taken, START_IN1 + 5)
                if ATT_STEP <= t < ATT_STEP + 8:
                    attention(t - ATT_STEP)
            out_projection(START_OUT1, mid_ready1, 6)
            ffn(START_FF1, M_FF1, 3, 7)

        @block.scalar
        def _(act):
            ck = Clock(act, s_act)

            def split(i, blk=0, per=0, between=None):
                for pc in range(PIECES):
                    wait(act, s_raw[pc], 16 * (i + 1), blk, 16 * per)
                    if i >= 2:
                        wait(act, s_mul, (i - 2) * PIECES + pc + 1, blk, per * PIECES)
                    o = ((i % 2) * PIECES + pc) * PW
                    act.activation(w_hi[:, o:o + PW], raw[:, pc * PW:(pc + 1) * PW], ACT.Copy).then_inc(s_hi, 1)
                    if pc == 1 and between:
                        between()

            def inverse_rms(n, dst, done):
                act.wait_ge(s_stat, n)
                ck.link(act.activation(dst, stat[:, 0:SEQ], ACT.Ln, scale=1.0 / D, bias=eps))
                act.activation(dst, dst, ACT.Exp, scale=-0.5).then_inc(done, 1)

            def next_input(phase):
                for k in range(KT):
                    if phase == 0:
                        if k == 0:
                            act.wait_ge(s_x, 16)
                            act.wait_ge(s_vec, 16)
                    else:
                        act.wait_ge(s_xn, (phase - 1) * KT + k + 1)
                    act.activation(tile(in_hi, k), tile(x, k), ACT.Copy,
                                   scale=vcol(V_NORM + 2 * phase * KT + k)).then_inc(s_inh, 1)
                last = act.activation(y[:, :], x[:, :], ACT.Square)
                last.then_inc(s_xsq, 1)

            def hidden(i, t, blk=0, per=0):
                wait(act, s_taken, i + 1, blk, per)
                ck.link(act.activation(g[:, :], u[:, :], ACT.Square))
                act.activation(tile(mid_hi, MT * t, MT), g[:, :], ACT.Copy).then_inc(s_g, 1)

            def squares(i, t):
                act.wait_ge(s_taken, i + 1)
                act.activation(g[:, :], tile(y, MT * t, MT), ACT.Square).then_inc(s_g, 1)

            def hgrn(n):
                b = tile(bb, n)
                b2 = v3(b, 2 * CHUNK)
                m3 = mm[:, 3 * SEQ:4 * SEQ]
                for grp in range(2):
                    act.wait_ge(s_dist, 2 * n + grp + 1)
                    ck.link(act.activation(mm[:, 0:3 * SEQ], mm[:, 0:3 * SEQ], ACT.Abs))
                    ins = act.activation(mm[:, 0:3 * SEQ], mm[:, 0:3 * SEQ], ACT.Exp, scale=-1.0)
                    if grp == 1:
                        act.activation(v3(m3, 2 * CHUNK)[:, :, CHUNK:], b2[:, :, CHUNK:], ACT.Exp)
                        for c in (0, 2):
                            ins = act.activation(m3[:, c * CHUNK:(c + 1) * CHUNK], b[:, c * CHUNK:(c + 1) * CHUNK], ACT.Exp,
                                                 scale=-1.0, bias=b[:, (c + 1) * CHUNK - 1:(c + 1) * CHUNK])
                    ins.then_inc(s_dec, 1)
                act.wait_ge(s_lv, 4 * n + 4)
                m0 = mm[:, 0:SEQ]
                for c, scale, bias in ((0, -1.0, tail2[:, n:n + 1]), (1, -1.0, b[:, 2 * CHUNK - 1:2 * CHUNK]),
                                       (2, 1.0, None), (3, 1.0, b[:, 3 * CHUNK - 1:3 * CHUNK])):
                    part = slice(c * CHUNK, (c + 1) * CHUNK)
                    if bias is None:
                        ins = act.activation(m0[:, part], b[:, part], ACT.Exp)
                    else:
                        ins = act.activation(m0[:, part], b[:, part], ACT.Exp, scale=scale, bias=bias)
                ins.then_inc(s_xdec, 1)
                act.wait_ge(s_oc, n + 1)
                act.activation(g[:, 0:SEQ], tile(qq, n), ACT.Square).then_inc(s_osq, 1)
                act.wait_ge(s_on, n + 1)
                ck.link(act.activation(g[:, 0:SEQ], stat[:, 0:SEQ], ACT.Ln, scale=1.0 / P, bias=eps))
                act.activation(g[:, 0:SEQ], g[:, 0:SEQ], ACT.Exp, scale=-0.5).then_inc(s_or, 1)

            def layernorm():
                act.wait_ge(s_cent, 1)
                for h in range(2):
                    if h:
                        act.wait_ge(s_lnsq, h)
                    act.activation(mm, tile(conv, 4 * h, 4), ACT.Square).then_inc(s_csq, 1)
                act.wait_ge(s_lnsq, 2)
                ck.link(act.activation(g[:, 0:SEQ], stat[:, SEQ:2 * SEQ], ACT.Ln, scale=1.0 / (A_TILES * P), bias=eps))
                act.activation(g[:, 0:SEQ], g[:, 0:SEQ], ACT.Exp, scale=-0.5).then_inc(s_lnr, 1)
                act.wait_ge(s_lnn, 1)
                for j in range(A_TILES):
                    ck.mark(act.activation(tile(conv, j), tile(conv, j), ACT.Identity, scale=vcol(V_LNW + j), bias=vcol(V_LNB + j)))
                ck.settle()
                for h in range(2):
                    if h:
                        act.wait_ge(s_lns, h)
                    act.activation(mm, tile(conv, 4 * h, 4), ACT.Sigmoid).then_inc(s_lna, 1)
                for h in range(2):
                    act.wait_ge(s_lns, h + 1)
                    act.activation(tile(mid_hi, 4 * h, 4), tile(conv, 4 * h, 4), ACT.Copy).then_inc(s_lnh, 1)

            def attention(r):
                c, gr = r // GROUPS, r % GROUPS
                n = CHUNK if c == 0 else WIN
                rows = slice(gr * DH, (gr + 1) * DH)
                act.wait_ge(s_sm, r + 1)
                act.activation(esink, esink, ACT.Exp)
                s4 = v3(sc, P)[:, :, 0:n]
                act.activation(s4, s4, ACT.Exp).then_inc(s_ex, 1)
                act.wait_ge(s_pt, r + 1)
                act.activation(pT[0:n, :], lev[1][0:n, :], ACT.Copy).then_inc(s_ptc, 1)
                act.wait_ge(s_pv, r + 1)
                act.activation(v3(dT, SEQ)[rows, :, c * CHUNK:(c + 1) * CHUNK], v3(misc[rows, :], CHUNK), ACT.Copy).then_inc(s_d, 1)

            act.wait_ge(s_eps, 1)
            split(0)
            next_input(0)

            act.wait_ge(s_lbx, 1)
            act.activation(small[:, 32:48], small[:, 32:48], ACT.Exp).then_inc(s_lbe, 1)
            def gated_high(j):
                act.wait_ge(s_gate, j + 1)
                act.activation(tile(mid_hi, 8 + 2 * j, 2), g[:, :], ACT.Copy).then_inc(s_gate_hi, 1)

            for t, (kind, j) in enumerate(IN0):
                split(t + 1, between=(lambda: gated_high(j - 1)) if kind == "g" and j else None)
                if t == 0:
                    inverse_rms(1, rpre[:, :], s_rpre)
                if kind in "afg":
                    act.wait_ge(s_taken, t + 1)
                    if kind == "a":
                        act.activation(g[:, 0:SEQ], u[:, SEQ:2 * SEQ], ACT.Sigmoid).then_inc(s_g, 1)
                    else:
                        act.activation(g[:, :], u[:, :], ACT.Sigmoid).then_inc(s_g, 1)
                if t == SCAN_STEP:
                    act.wait_ge(s_f, 4)
                    act.activation(bb, bb, ACT.Ln).then_inc(s_lnf, 1)
                if kind == "q":
                    hgrn(2 * j)
                    hgrn(2 * j + 1)
                if t == LN_STEP:
                    layernorm()
            gated_high(HEADS // 2 - 1)

            def out_projection(start):
                for t in range(OUT_TASKS):
                    split(start + t + 1)
                    squares(start + t, t)

            def ffn(start, n):
                per = 2 * BLOCK
                for t in range(BLOCK):
                    split(start + t + 1)
                    if t == 0:
                        inverse_rms(n, rpre[:, :], s_rpre)
                    hidden(start + t, t)
                for t in range(BLOCK):
                    split(start + BLOCK + t + 1)
                n0 = ck.n
                with act.Fori(1, FF_BLOCKS - 1) as blk:
                    ck.rt = (blk - 1) * BLOCK
                    for t in range(BLOCK):
                        split(start + t + 1, blk, per)
                        hidden(start + t, t, blk, per)
                    for t in range(BLOCK):
                        split(start + BLOCK + t + 1, blk, per)
                assert ck.n == n0 + BLOCK
                ck.rt, ck.n = 0, n0 + BLOCK * (FF_BLOCKS - 2)
                s2 = start + per * (FF_BLOCKS - 1)
                for t in range(BLOCK):
                    split(s2 + t + 1)
                    hidden(s2 + t, t)
                for t in range(BLOCK):
                    if s2 + BLOCK + t + 1 < TASKS:
                        split(s2 + BLOCK + t + 1)
                    squares(s2 + BLOCK + t, t)

            out_projection(START_OUT0)
            inverse_rms(2, rpost[:, :], s_rpost)
            next_input(1)
            ffn(START_FF0, 3)
            inverse_rms(4, rpost[:, :], s_rpost)
            next_input(2)

            for t, (kind, j) in enumerate(IN1):
                split(START_IN1 + t + 1)
                if t == 0:
                    inverse_rms(5, rpre[:, :], s_rpre)
                if ATT_STEP <= t < ATT_STEP + 8:
                    attention(t - ATT_STEP)
                if t == ATT_STEP + 8:
                    act.wait_ge(s_d, 2 * SEQ // CHUNK)
                    act.activation(tile(mid_hi, 8, 8), dT, ACT.Copy).then_inc(s_dhi, 1)
                if kind == "c" and j % 3:
                    n = 2 * (j // 3) + (j % 3 - 1)
                    act.wait_ge(s_c, n + 1)
                    act.activation(tile(mid_hi, n), cacc, ACT.Copy).then_inc(s_chi, 1)

            out_projection(START_OUT1)
            inverse_rms(6, rpost[:, :], s_rpost)
            next_input(3)
            ffn(START_FF1, 7)
            inverse_rms(8, rpost[:, :], s_rpost)

        @block.vector
        def _(dve):
            ck = Clock(dve, s_dve)

            def split(i, blk=0, per=0, between=None):
                for pc in range(PIECES):
                    wait(dve, s_hi, i * PIECES + pc + 1, blk, per * PIECES)
                    o = ((i % 2) * PIECES + pc) * PW
                    dve.tensor_tensor(w_lo[:, o:o + PW], raw[:, pc * PW:(pc + 1) * PW], w_hi[:, o:o + PW],
                                      ALU.subtract).then_inc(s_lo, 1)
                    if pc == 1 and between:
                        between()

            def result(i, blk=0, per=0):
                wait(dve, s_mul, (i + 1) * PIECES, blk, per * PIECES)
                return v3(dense_bank[i % 4][:, :], SEQ)

            def scaled(dst, i):
                return dve.tensor_tensor(v3(dst, SEQ), result(i), per_token(rpre[:, :], MT), ALU.mult)

            def next_input(phase):
                if phase == 0:
                    dve.wait_ge(s_vec, 16)
                for k in range(KT):
                    if phase > 0:
                        dve.wait_ge(s_yr, (phase - 1) * KT + k + 1)
                        dve.scalar_tensor_tensor(out=tile(x, k), in0=tile(y, k), scalar=vcol(V_NORM + (2 * phase - 1) * KT + k),
                                                 in1=tile(x, k), op0=ALU.mult, op1=ALU.add).then_inc(s_xn, 1)
                    if phase < 4:
                        dve.wait_ge(s_inh, phase * KT + k + 1)
                        dve.scalar_tensor_tensor(out=tile(in_lo, k), in0=tile(x, k), scalar=vcol(V_NORM + 2 * phase * KT + k),
                                                 in1=tile(in_hi, k), op0=ALU.mult, op1=ALU.subtract).then_inc(s_inl, 1)

            def x_sum(n):
                dve.wait_ge(s_xsq, n)
                dve.tensor_reduce(sqsum[:, :], y[:, :].rearrange("p (k t) -> p t k", k=KT), AX_X, ALU.add).then_inc(s_sum, 1)

            dve.memset(small[:, :], EPS).then_inc(s_eps, 1)
            ck.link(dve.memset(hpad[:, :], 0.0))
            split(0)
            next_input(0)
            l0, l1 = vec[:, V_LB:V_LB + HEADS], vec[:, V_LB + HEADS:V_LB + 2 * HEADS]
            e0, e1, top = small[:, 32:40], small[:, 40:48], small[:, 48:56]
            ck.link(dve.tensor_tensor(top, l0, l1, ALU.max))
            ck.link(dve.tensor_tensor(e0, l0, top, ALU.subtract))
            dve.tensor_tensor(e1, l1, top, ALU.subtract).then_inc(s_lbx, 1)
            dve.wait_ge(s_lbe, 1)
            ck.link(dve.tensor_tensor(top, e0, e1, ALU.add))
            ck.link(dve.reciprocal(top, top))
            ck.link(dve.tensor_tensor(lb, e0, top, ALU.mult))
            ck.link(dve.tensor_scalar(omlb, lb, -1.0, 1.0, ALU.mult, ALU.add))
            x_sum(1)

            def late0(t):
                if t < 0 or IN0[t][0] not in "afg":
                    return
                kind, j = IN0[t]
                dve.wait_ge(s_g, G0[t])
                if kind == "a":
                    o = (j % 2) * (SEQ + A_CONV - 1) + A_CONV - 1
                    ck.link(dve.tensor_tensor(hpad[:, o:o + SEQ], u[:, 0:SEQ], g[:, 0:SEQ], ALU.mult))
                elif kind == "f":
                    for m in range(MT):
                        n = 2 * j + m
                        ck.mark(dve.tensor_scalar(tile(bb, n), tile(g, m), omlb[:, n:n + 1], lb[:, n:n + 1], ALU.mult, ALU.add))
                    ck.settle()
                    dve.tensor_scalar(tile(kk, 2 * j, 2), tile(bb, 2 * j, 2), -1.0, 1.0, ALU.mult, ALU.add).then_inc(s_f, 1)
                else:
                    ck.link(dve.tensor_tensor(g[:, :], u[:, :], g[:, :], ALU.mult))
                    dve.tensor_tensor(g[:, :], g[:, :], tile(qq, 2 * j, 2), ALU.mult).then_inc(s_gate, 1)
                    dve.wait_ge(s_gate_hi, j + 1)
                    dve.tensor_tensor(tile(mid_lo, 8 + 2 * j, 2), g[:, :], tile(mid_hi, 8 + 2 * j, 2), ALU.subtract).then_inc(s_mid, 1)

            def hgrn(n):
                b, k, q = tile(bb, n), tile(kk, n), tile(qq, n)

                def decayed(m, half, last):
                    m3, k3, q3 = (v3(z, 2 * half) for z in (m, k, q))
                    ck.mark(dve.tensor_tensor(m3[:, :, 0:half], m3[:, :, 0:half], k3[:, :, 0:half], ALU.mult))
                    ins = dve.tensor_tensor(m3[:, :, half:], m3[:, :, half:], q3[:, :, half:], ALU.mult)
                    if last:
                        ins.then_inc(s_kq, 1)
                    else:
                        ck.mark(ins)

                def levels(grp, tt):
                    dve.wait_ge(s_lv, 4 * n + 2 * grp + tt + 1)
                    tmp = (u, g)[tt][:, :]
                    ck.link(dve.tensor_tensor(tmp, lev[tt][:, :], con[:, C_MASK + grp * 4 * P:C_MASK + (grp + 1) * 4 * P], ALU.mult))
                    t3 = tmp.rearrange("p (l t) -> p t l", l=4)
                    dst = pairs[:, tt * P:(tt + 1) * P]
                    if grp == 0:
                        ck.link(dve.tensor_reduce(dst, t3, AX_X, ALU.add))
                    else:
                        ck.link(dve.tensor_reduce(acc2[:, 0:P], t3, AX_X, ALU.add))
                        ck.link(dve.tensor_tensor(dst, dst, acc2[:, 0:P], ALU.add))

                for grp, halves in ((0, HALVES[1:4]), (1, HALVES[4:7])):
                    for l, half in enumerate(halves):
                        m3, b3 = v3(mm[:, l * SEQ:(l + 1) * SEQ], 2 * half), v3(b, 2 * half)
                        ref = b3[:, :, half - 1:half].to_broadcast([P, SEQ // (2 * half), 2 * half])
                        ins = dve.tensor_tensor(m3, b3, ref, ALU.subtract)
                        if l == 2:
                            ins.then_inc(s_dist, 1)
                        else:
                            ck.mark(ins)
                    dve.wait_ge(s_dec, 2 * n + grp + 1)
                    for l, half in enumerate(halves):
                        decayed(mm[:, l * SEQ:(l + 1) * SEQ], half, grp == 0 and l == 2)
                    if grp:
                        decayed(mm[:, 3 * SEQ:4 * SEQ], CHUNK, True)
                    levels(grp, 0)
                    levels(grp, 1)
                dve.wait_ge(s_xdec, n + 1)
                decayed(mm[:, 0:SEQ], P, True)
                dve.wait_ge(s_xp, n + 1)
                dve.tensor_copy(pairs[:, 2 * P:3 * P], misc[:, 2 * P:3 * P]).then_inc(s_pairs, 1)
                dve.wait_ge(s_o, n + 1)
                dve.tensor_copy(q, misc[:, 0:SEQ]).then_inc(s_oc, 1)
                dve.wait_ge(s_or, n + 1)
                ck.link(dve.scalar_tensor_tensor(out=q, in0=q, scalar=vcol(V_BN), in1=g[:, 0:SEQ], op0=ALU.mult, op1=ALU.mult))

            def layernorm():
                ck.settle()
                dve.tensor_scalar(small[:, 56:57], eps, 0.0, None, ALU.mult).then_inc(s_conv, 1)
                dve.wait_ge(s_lnsum, 1)
                c3 = v3(conv, SEQ)
                ck.link(dve.tensor_scalar(acc2[:, :], stat[:, 0:SEQ], 1.0 / (A_TILES * P), None, ALU.mult))
                dve.tensor_tensor(c3, c3, per_token(acc2[:, :], A_TILES), ALU.subtract).then_inc(s_cent, 1)
                dve.wait_ge(s_lnr, 1)
                dve.tensor_tensor(c3, c3, per_token(g[:, 0:SEQ], A_TILES), ALU.mult).then_inc(s_lnn, 1)
                for h in range(2):
                    dve.wait_ge(s_lna, h + 1)
                    dve.tensor_tensor(tile(conv, 4 * h, 4), tile(conv, 4 * h, 4), mm, ALU.mult).then_inc(s_lns, 1)
                for h in range(2):
                    dve.wait_ge(s_lnh, h + 1)
                    dve.tensor_tensor(tile(mid_lo, 4 * h, 4), tile(conv, 4 * h, 4), tile(mid_hi, 4 * h, 4),
                                      ALU.subtract).then_inc(s_mid, 2)

            def attention(r):
                c, gr = r // GROUPS, r % GROUPS
                n = CHUNK if c == 0 else WIN
                s4, b4 = v3(sc, P)[:, :, 0:n], v3(wk[:, gr * 512:(gr + 1) * 512], P)[:, :, WIN - n:]
                sink = vec[:, V_SINK + 4 * gr:V_SINK + 4 * gr + 4]

                def per_row(a):
                    return a.unsqueeze(2).to_broadcast([P, 4, n])

                dve.wait_ge(s_sc, r + 1)
                ck.link(dve.tensor_tensor(s4, v3(lev[0][:, :], P)[:, :, 0:n], b4, ALU.add))
                ck.link(dve.tensor_reduce(mx, s4, AX_X, ALU.max))
                ck.link(dve.tensor_tensor(mx, mx, sink, ALU.max))
                ck.mark(dve.tensor_tensor(esink, sink, mx, ALU.subtract))
                dve.tensor_tensor(s4, s4, per_row(mx), ALU.subtract).then_inc(s_sm, 1)
                dve.wait_ge(s_ex, r + 1)
                ck.link(dve.tensor_reduce(den, s4, AX_X, ALU.add))
                ck.link(dve.tensor_tensor(den, den, esink, ALU.add))
                ck.link(dve.reciprocal(rden, den))
                dve.tensor_tensor(s4, s4, per_row(rden), ALU.mult).then_inc(s_p, 1)

            def taps(j, part):
                h = hpad[:, (j % 2) * (SEQ + A_CONV - 1):(j % 2 + 1) * (SEQ + A_CONV - 1)]
                a = tile(conv, j)
                half = 16
                for q in (range(half) if part == 0 else range(half, A_CONV)):
                    wq = vcol(V_DW + j * A_CONV + q)
                    dst = a if q % 2 == 0 else acc2[:, :]
                    if q == 0:
                        ck.mark(dve.tensor_scalar(dst, h[:, 0:SEQ], wq, vcol(V_DWB + j), ALU.mult, ALU.add))
                    elif q == 1:
                        ck.mark(dve.tensor_scalar(dst, h[:, 1:1 + SEQ], wq, None, ALU.mult))
                    else:
                        ck.settle(1)
                        ck.mark(dve.scalar_tensor_tensor(out=dst, in0=h[:, q:q + SEQ], scalar=wq, in1=dst,
                                                         op0=ALU.mult, op1=ALU.add))
                ck.settle()
                if part == 1:
                    ck.link(dve.tensor_tensor(a, a, acc2[:, :], ALU.add))

            for t, (kind, j) in enumerate(IN0):
                split(t + 1, between=lambda: late0(t - 1))
                if t == 0:
                    dve.wait_ge(s_rpre, 1)
                dst = u[:, :] if kind in "afg" else tile(qq, 2 * j, 2)
                scaled(dst, t).then_inc(s_taken, 1)
                dve.wait_ge(s_taken, t + 1)
                before = IN0[t - 1] if t else ("", 0)
                if before[0] == "i":
                    dve.wait_ge(s_vt, before[1] + 1)
                    for m in range(MT):
                        h0 = (2 * before[1] + m) * P
                        ck.link(dve.tensor_copy(v3(vtok, HEADS * P)[:, :, h0:h0 + P], v3(misc[:, m * 2 * P:(m + 1) * 2 * P], P)))
                if before[0] == "a":
                    taps(before[1], 0)
                if t >= 2 and IN0[t - 2][0] == "a":
                    taps(IN0[t - 2][1], 1)
                if t == SCAN_STEP:
                    dve.wait_ge(s_lnf, 1)
                    for n in range(HEADS):
                        ck.mark(dve.tensor_tensor_scan(tile(bb, n), con[:, C_RESET:C_RESET + SEQ], tile(bb, n), 0.0,
                                                       ALU.mult, ALU.add))
                    ck.settle()
                    b3 = v3(bb, SEQ)
                    dve.tensor_tensor(tail2.unsqueeze(2), b3[:, :, CHUNK - 1:CHUNK], b3[:, :, 2 * CHUNK - 1:2 * CHUNK],
                                      ALU.add).then_inc(s_scan, 1)
                if kind == "q":
                    hgrn(2 * j)
                    hgrn(2 * j + 1)
                if t == LN_STEP:
                    layernorm()
            late0(len(IN0) - 1)

            def add_squares(ui):
                dve.wait_ge(s_g, ui + 1)
                ck.link(dve.tensor_tensor(sqsum[:, :], sqsum[:, :], g[:, 0:SEQ], ALU.add))
                ins = dve.tensor_tensor(sqsum[:, :], sqsum[:, :], g[:, SEQ:2 * SEQ], ALU.add)
                return ins

            def finish_squares(ui):
                add_squares(ui).then_inc(s_sum, 1)

            def out_projection(start, gi):
                ck.link(dve.memset(sqsum[:, :], 0.0))
                for t in range(OUT_TASKS):
                    split(start + t + 1, between=(lambda: ck.link(add_squares(gi + t - 1))) if t else None)
                    dve.tensor_copy(v3(tile(y, MT * t, MT), SEQ), result(start + t)).then_inc(s_taken, 1)
                finish_squares(gi + OUT_TASKS - 1)

            def up(i, blk=0, per=0):
                dve.scalar_tensor_tensor(out=v3(u[:, :], SEQ), in0=result(i, blk, per), scalar=0.0,
                                         in1=per_token(rpre[:, :], MT), op0=ALU.max, op1=ALU.mult).then_inc(s_taken, 1)

            def low_hidden(gi, t, blk=0, per=0):
                wait(dve, s_g, gi + 1, blk, per)
                dve.tensor_tensor(tile(mid_lo, MT * t, MT), g[:, :], tile(mid_hi, MT * t, MT), ALU.subtract).then_inc(s_mid, 1)

            def down(i, t, first=False, blk=0, per=0):
                r = result(i, blk, per)
                dst = v3(tile(y, MT * t, MT), SEQ)
                ins = dve.tensor_copy(dst, r) if first else dve.tensor_tensor(dst, r, dst, ALU.add)
                ins.then_inc(s_taken, 1)

            def ffn(start, gi, n):
                per = 2 * BLOCK
                x_sum(n)

                def ups(s0, g0, blk=0):
                    p, q = (per, BLOCK) if not isinstance(blk, int) else (0, 0)
                    for t in range(BLOCK):
                        split(s0 + t + 1, blk, p, between=(lambda: low_hidden(g0 + t - 1, t - 1, blk, q)) if t else None)
                        if s0 == start and t == 0:
                            dve.wait_ge(s_rpre, n)
                        up(s0 + t, blk, p)
                    return lambda: low_hidden(g0 + BLOCK - 1, BLOCK - 1, blk, q)

                left = ups(start, gi)
                for t in range(BLOCK):
                    split(start + BLOCK + t + 1, between=left if t == 0 else None)
                    down(start + BLOCK + t, t, first=True)
                with dve.Fori(1, FF_BLOCKS - 1) as blk:
                    left = ups(start, gi, blk)
                    for t in range(BLOCK):
                        split(start + BLOCK + t + 1, blk, per, between=left if t == 0 else None)
                        down(start + BLOCK + t, t, blk=blk, per=per)
                s2, g2 = start + per * (FF_BLOCKS - 1), gi + BLOCK * (FF_BLOCKS - 1)
                left = ups(s2, g2)
                ck.link(dve.memset(sqsum[:, :], 0.0))
                for t in range(BLOCK):
                    i = s2 + BLOCK + t
                    between = left if t == 0 else (lambda: ck.link(add_squares(g2 + BLOCK + t - 1)))
                    if i + 1 < TASKS:
                        split(i + 1, between=between)
                    else:
                        between()
                    down(i, t)
                finish_squares(g2 + 2 * BLOCK - 1)

            out_projection(START_OUT0, G_OUT0)
            dve.wait_ge(s_back, 16)
            next_input(1)
            ffn(START_FF0, G_FF0, 2)
            next_input(2)

            x_sum(3)
            for t, (kind, j) in enumerate(IN1):
                i = START_IN1 + t
                split(i + 1)
                if t == 0:
                    dve.wait_ge(s_rpre, 3)
                    dve.wait_ge(s_spill, 16)
                if kind == "kv":
                    scaled(x[:, 0:512], i).then_inc(s_taken, 1)
                elif kind == "q":
                    r = result(i)
                    for m in range(MT):
                        dst = v3(qT, C_TILES * CHUNK)[:, :, (2 * j + m) * CHUNK:(2 * j + m + 1) * CHUNK]
                        ins = dve.scalar_tensor_tensor(out=dst, in0=v3(r[:, m, :], CHUNK), scalar=DH ** -0.5,
                                                       in1=v3(rpre[:, :], CHUNK), op0=ALU.mult, op1=ALU.mult)
                    ins.then_inc(s_taken, 1)
                else:
                    scaled(tile(cbuf, 2 * (j % 3), 2), i).then_inc(s_taken, 1)
                dve.wait_ge(s_taken, i + 1)
                if t == 1:
                    dve.wait_ge(s_win, 1)
                    ck.link(dve.tensor_copy(vwin, misc[:, 0:3 * P]))
                    ck.link(dve.memset(cpad, 0.0))
                if t == ATT_STEP:
                    dve.wait_ge(s_bias, 16)
                if ATT_STEP <= t < ATT_STEP + 8:
                    attention(t - ATT_STEP)
                if t == ATT_STEP + 8:
                    dve.wait_ge(s_dhi, 1)
                    dve.wait_ge(s_d, 2 * SEQ // CHUNK)
                    dve.tensor_tensor(tile(mid_lo, 8, 8), dT, tile(mid_hi, 8, 8), ALU.subtract).then_inc(s_dlo, 1)
                if kind == "c" and j % 3:
                    n = 2 * (j // 3) + (j % 3 - 1)
                    hh, cc, gb = ((0, 1, 2), (3, 4, 5))[j % 3 - 1]
                    ck.link(dve.tensor_tensor(cpad[:, 2:2 + SEQ], tile(cbuf, hh), tile(cbuf, cc), ALU.mult))
                    for q in range(C_CONV):
                        wq = vcol(V_CC + n * C_CONV + q)
                        if q == 0:
                            ck.link(dve.tensor_scalar(cacc, cpad[:, 0:SEQ], wq, None, ALU.mult))
                        else:
                            ck.link(dve.scalar_tensor_tensor(out=cacc, in0=cpad[:, q:q + SEQ], scalar=wq, in1=cacc,
                                                             op0=ALU.mult, op1=ALU.add))
                    dve.tensor_tensor(cacc, cacc, tile(cbuf, gb), ALU.mult).then_inc(s_c, 1)
                    dve.wait_ge(s_chi, n + 1)
                    ins = dve.tensor_tensor(tile(mid_lo, n), cacc, tile(mid_hi, n), ALU.subtract)
                    if n % 2:
                        ins.then_inc(s_mid, 1)
                    else:
                        ck.link(ins)

            out_projection(START_OUT1, G_OUT1)
            dve.wait_ge(s_back, 32)
            next_input(3)
            ffn(START_FF1, G_FF1, 4)
            next_input(4)


def _tiles(v):
    v = np.asarray(v)
    return v.reshape(v.shape[:-1] + (v.shape[-1] // P, P))


def _columns():
    r = np.arange(P)
    aw, hw = A_TILES * P, HEADS * P
    base = {"f": 2 * aw + hw, "q": 2 * aw, "i": 2 * aw + 2 * hw, "g": 2 * aw + 3 * hw}
    in0 = []
    for kind, j in IN0:
        if kind == "a":
            in0.append(np.concatenate([j * P + r, aw + j * P + r]))
        else:
            in0.append(base[kind] + 2 * j * P + np.arange(2 * P))
    cw = C_TILES * P
    qb, kb = 3 * cw, 3 * cw + Q_HEADS * DH
    in1 = []
    d = np.arange(DH)
    order = []
    for j in range(C_TILES // 2):
        order += [(0, 2 * j), (2, 2 * j), (1, 2 * j), (0, 2 * j + 1), (2, 2 * j + 1), (1, 2 * j + 1)]
    for kind, j in IN1:
        if kind == "kv":
            in1.append(kb + np.arange(2 * P))
        elif kind == "q":
            in1.append(np.concatenate([qb + h * DH + d for n in (2 * j, 2 * j + 1) for h in (n, Q_HEADS // 2 + n)]))
        else:
            in1.append(np.concatenate([part * cw + n * P + r for part, n in order[2 * j:2 * j + 2]]))
    return np.concatenate(in0), np.concatenate(in1)


def _head_rows():
    d = np.arange(DH)
    return np.concatenate([h * DH + d for n in range(Q_HEADS // 2) for h in (n, Q_HEADS // 2 + n)])


def _stream(parts):
    out = np.empty((TASKS, P, KT, COLS), np.float32)
    at = 0
    for m in parts:
        n = m.shape[1] // COLS
        out[at:at + n] = m.reshape(KT, P, n, COLS).transpose(2, 1, 0, 3)
        at += n
    assert at == TASKS
    return out.reshape(TASKS, P, KT * COLS)


def _constants():
    con = np.zeros((P, C_N), np.float32)
    con[:, C_ID:C_ID + P] = np.eye(P)
    con[:, C_ONE:C_ONE + P] = 1
    s, t = np.arange(P)[:, None], np.arange(P)[None, :]
    for l, half in enumerate(HALVES):
        if half == 0:
            m = s == t
        else:
            m = (s // (2 * half) == t // (2 * half)) & (s % (2 * half) < half) & (t % (2 * half) >= half)
        con[:, C_MASK + l * P:C_MASK + (l + 1) * P] = m
    con[:, C_RESET:C_RESET + SEQ] = (np.arange(SEQ) % CHUNK != 0)
    slopes = (2.0 ** (-8.0 * np.arange(1, Q_HEADS + 1, dtype=np.float32) / Q_HEADS)).astype(np.float32)
    dist = np.abs(np.arange(CHUNK)[:, None] + CHUNK - np.arange(WIN)[None, :]).astype(np.float32)
    bias = np.zeros((2, CHUNK, GROUPS, 4, WIN), np.float32)
    for gr in range(GROUPS):
        for jp in range(4):
            for e in range(2):
                bias[e, :, gr, jp, :] = -slopes[8 * gr + 2 * jp + e] * dist
    return con, bias.reshape(P, GROUPS * 4 * WIN)


def kernel(x, w_in_even, w_out_even, a_dw_w, a_dw_b, a_ln_w, a_ln_b, b_lb_logits, b_norm_w, w_in_odd, w_out_odd,
           c_conv_w, d_sinks, norm_pre_mix, norm_post_mix, norm_pre_ffn, norm_post_ffn, w_ffn_up, w_ffn_down):
    import concourse.bacc as bacc
    from concourse.bass_utils import run_bass_kernel_spmd

    cols0, cols1 = _columns()
    rows1 = np.concatenate([np.arange(C_TILES * P), C_TILES * P + _head_rows()])

    def ffn(l):
        up, down = np.asarray(w_ffn_up)[l], np.asarray(w_ffn_down)[l]
        return [m for b in range(FF_BLOCKS) for m in (up[:, b * D:(b + 1) * D], down[b * D:(b + 1) * D])]

    stream = _stream([np.asarray(w_in_even)[0][:, cols0], np.asarray(w_out_even)[0], *ffn(0),
                      np.asarray(w_in_odd)[0][:, cols1], np.asarray(w_out_odd)[0][rows1], *ffn(1)])
    vec = np.empty((P, V_N), np.float32)
    norms = [np.asarray(v)[l] for l in range(2) for v in (norm_pre_mix, norm_post_mix, norm_pre_ffn, norm_post_ffn)]
    for n, v in enumerate(norms):
        vec[:, V_NORM + n * KT:V_NORM + (n + 1) * KT] = _tiles(v).T
    vec[:, V_DW:V_DWB] = _tiles(a_dw_w[0]).transpose(2, 1, 0).reshape(P, A_TILES * A_CONV)
    vec[:, V_DWB:V_LNW] = _tiles(a_dw_b[0]).T
    vec[:, V_LNW:V_LNB] = _tiles(a_ln_w[0]).T
    vec[:, V_LNB:V_LB] = _tiles(a_ln_b[0]).T
    vec[:, V_LB:V_BN] = _tiles(b_lb_logits).transpose(2, 0, 1).reshape(P, 2 * HEADS)
    vec[:, V_BN] = np.asarray(b_norm_w)[0]
    vec[:, V_CC:V_SINK] = _tiles(c_conv_w[0]).transpose(2, 1, 0).reshape(P, C_TILES * C_CONV)
    sinks = np.asarray(d_sinks)[0].reshape(GROUPS, 4, 2)
    vec[:, V_SINK:] = np.repeat(sinks.transpose(2, 0, 1).reshape(2, 1, 8), CHUNK, axis=1).reshape(P, 8)
    con, bias = _constants()
    xt = np.ascontiguousarray(np.asarray(x)[0].T.reshape(KT, P, SEQ).transpose(1, 0, 2)).reshape(P, KT * SEQ)

    arrays = {"weights": stream, "x_in": xt, "vectors": vec, "constants": con, "alibi": bias}
    nc = bacc.Bacc("TRN2", target_bir_lowering=False, num_devices=1)
    ins = [nc.dram_tensor(k, a.shape, F32, kind="ExternalInput").ap() for k, a in arrays.items()]
    xsave = nc.dram_tensor("x_save", (P, KT * SEQ), F32, kind="Internal").ap()
    out = nc.dram_tensor("out", (P, KT * SEQ), F32, kind="ExternalOutput").ap()
    bass_hybrid_trunk(nc, *ins, xsave, out)
    r = run_bass_kernel_spmd(nc, [arrays], core_ids=[0])
    got = r.results[0]["out"]
    return np.ascontiguousarray(got.reshape(P, KT, SEQ).transpose(2, 1, 0)).reshape(1, SEQ, D)
```

```python
from contextlib import ExitStack

import numpy as np

import concourse.bass as bass
from concourse import mybir

F32 = mybir.dt.float32
F32R = mybir.dt.float32r
ALU = mybir.AluOpType
ACT = mybir.ActivationFunctionType
AX_X = mybir.AxisListType.X

P = 128
SEQ = 256
D = 2048
KT = D // P
FF = 4 * D
COLS = 256
MT = COLS // P
PIECES = 4
KP = KT // PIECES
PW = KP * COLS
EPS = 1e-6

A_TILES = 8
A_CONV = 31
HEADS = 8
CHUNK = 64
C_TILES = 8
C_CONV = 3
Q_HEADS, GROUPS, DH = 16, 2, 64
WIN = 128

IN0 = [x for n in range(4) for x in (("a", 2 * n), ("a", 2 * n + 1), ("f", n), ("q", n), ("i", n))] + \
      [("g", n) for n in range(4)]
IN1 = [("kv", 0)] + [("q", j) for j in range(4)] + [("c", j) for j in range(12)]
OUT_TASKS = D // COLS
BLOCK = D // COLS
FF_BLOCKS = FF // D
START_IN0 = 0
START_OUT0 = START_IN0 + len(IN0)
START_FF0 = START_OUT0 + OUT_TASKS
START_IN1 = START_FF0 + 2 * BLOCK * FF_BLOCKS
START_OUT1 = START_IN1 + len(IN1)
START_FF1 = START_OUT1 + OUT_TASKS
TASKS = START_FF1 + 2 * BLOCK * FF_BLOCKS

V_NORM = 0
V_DW = V_NORM + 8 * KT
V_DWB = V_DW + A_TILES * A_CONV
V_LNW = V_DWB + A_TILES
V_LNB = V_LNW + A_TILES
V_LB = V_LNB + A_TILES
V_BN = V_LB + 2 * HEADS
V_CC = V_BN + 1
V_SINK = V_CC + C_TILES * C_CONV
V_N = V_SINK + Q_HEADS // 2
T_DVE, T_DVE_LAST = 4, 8


def pieces_after(phase, k):
    return ({KT - 1: (0, 1, 2, 3)} if phase == 0 else {7: (0, 1), KT - 1: (2, 3)}).get(k, ())


HBUF = 4

def after_task(kind, j, tasks):
    return PIECES * (tasks.index((kind, j)) + 1)


HEAD_GAP = 9
HEAD_TICK = [after_task("q", n // 2, IN0) + HEAD_GAP * (n % 2) for n in range(HEADS)]
SCAN_TICK = [after_task("f", j, IN0) + 2 for j in range(HEADS // 2)]
TAPS = 4
CONV_TICKS = -(-A_CONV // TAPS)
CONV_TICK = []
for _j in range(A_TILES):
    CONV_TICK.append(max(after_task("a", _j, IN0) + 2, CONV_TICK[-1] + CONV_TICKS if _j else 0))
NORM_TICK = CONV_TICK[-1] + CONV_TICKS
ATT_TICK = [after_task("q", 3, IN1) + 5 * r for r in range(GROUPS * SEQ // CHUNK)]
ATT_END = ATT_TICK[-1] + 5

HALVES = [0, 1, 2, 4, 8, 16, 32]
LEVELS = len(HALVES)
C_ID = 0
C_ONE = C_ID + P
C_MASK = C_ONE + P
C_RESET = C_MASK + LEVELS * CHUNK
C_N = C_RESET + SEQ



class Clock:

    def __init__(self, eng, sem):
        self.eng, self.sem, self.n, self.rt = eng, sem, 0, 0

    def mark(self, ins):
        self.n += 1
        ins.then_inc(self.sem, 1)

    def settle(self, back=0):
        if self.n > back:
            self.eng.wait_ge(self.sem, self.rt + (self.n - back))

    def link(self, ins):
        self.mark(ins)
        self.settle()


def bass_hybrid_trunk(nc: bass.Bass, w, xin, vecs, consts, bias, xsave, out):
    with ExitStack() as ctx:
        def sb(name, cols, dt=F32):
            return ctx.enter_context(nc.sbuf_tensor(name, [P, cols], dt))

        def sem(name):
            return ctx.enter_context(nc.semaphore(name))

        raw = sb("raw", PIECES * PW)
        w_hi = sb("w_hi", 2 * PIECES * PW, F32R)
        w_lo = sb("w_lo", 2 * PIECES * PW, F32R)
        in_hi = sb("in_hi", KT * SEQ, F32R)
        in_lo = sb("in_lo", KT * SEQ, F32R)
        mid_at = -(-nc.sbuf_base // 32) * 32
        spare = sb("spare", 2 * KT * SEQ)
        assert nc.sbuf_base == mid_at + 4 * 2 * KT * SEQ
        mid_hi = nc.alloc_sbuf_tensor_at("mid_hi", [P, KT * SEQ], F32R, offset=mid_at)
        mid_lo = nc.alloc_sbuf_tensor_at("mid_lo", [P, KT * SEQ], F32R, offset=mid_at + 4 * KT * SEQ)
        x = sb("x", KT * SEQ)
        y = sb("y", KT * SEQ)
        vec = sb("vec", V_N)
        con = sb("con", C_N)
        rpre = sb("rpre", SEQ)
        rpost = sb("rpost", SEQ)
        sqsum = sb("sqsum", SEQ)
        u = sb("u", MT * SEQ)
        g = sb("g", MT * SEQ)
        wk = sb("wk", 3072)
        acc2 = sb("acc2", SEQ)
        pairs = sb("pairs", 3 * P)
        small = sb("small", 64)

        dense_bank = [ctx.enter_context(nc.psum_tensor(f"dense{n}", [P, 512], F32)) for n in range(4)]
        stat, misc = (ctx.enter_context(nc.psum_tensor(n, [P, 512], F32)) for n in ("stat", "misc"))
        levels = ctx.enter_context(nc.psum_tensor("levels", [P, 1024], F32))
        lev = [levels[:, 0:512], levels[:, 512:1024]]

        ident = con[:, C_ID:C_ID + P]
        ones = con[:, C_ONE:C_ONE + P]
        eps = small[:, 0:1]
        lb, omlb = small[:, 8:16], small[:, 16:24]
        tail2 = small[:, 24:32]
        mx, esink, den, rden = small[:, 32:36], small[:, 36:40], small[:, 40:44], small[:, 44:48]

        conv, kk = x[:, 0:2048], x[:, 2048:4096]
        bb, qq = y[:, 0:2048], y[:, 2048:4096]
        vtok, lnsq = wk[:, 0:2048], wk[:, 2048:3072]
        mm = [spare[:, l * SEQ:(l + 1) * SEQ] for l in range(7)]
        mx_cross = spare[:, 4096:4096 + SEQ]
        HP = SEQ + A_CONV - 1
        hpad = spare[:, 4096 + SEQ:4096 + SEQ + HBUF * HP]
        masked, msum = spare[:, 3072:3072 + 2 * 7 * CHUNK], spare[:, 3072 + 896:4096]
        kT, vT, vwin = x[:, 0:256], x[:, 256:512], x[:, 512:896]
        sc, pT = x[:, 896:1408], x[:, 1408:1920]
        cbuf, cpad, cacc = x[:, 1920:3456], x[:, 3456:3456 + SEQ + 2], x[:, 3714:3970]
        qT, dT = y[:, 0:2048], y[:, 2048:4096]

        def v3(ap, c):
            return ap.rearrange("p (a b) -> p a b", b=c)

        def per_token(ap, n):
            return ap.unsqueeze(1).to_broadcast([P, n, SEQ])

        def tile(ap, k, n=1):
            return ap[:, k * SEQ:(k + n) * SEQ]

        def vcol(c):
            return vec[:, c:c + 1]

        s_vec, s_con, s_bias = sem("vectors_landed"), sem("constants_landed"), sem("bias_landed")
        s_back, s_spill, s_out = sem("x_back"), sem("x_spilled"), sem("out_written")
        s_x = [sem(f"x{n}_landed") for n in range(PIECES)]
        s_raw = [sem(f"piece{n}_landed") for n in range(PIECES)]
        s_hi, s_lo, s_mul = sem("weights_high"), sem("weights_split"), sem("pieces_multiplied")
        s_taken = sem("results_taken")
        s_pool = sem("pool_clock")
        s_act, s_dve = sem("act_clock"), sem("dve_clock")
        s_xn, s_inh, s_inl = sem("x_updated"), sem("input_high"), sem("input_split")
        s_xsq, s_sum, s_stat, s_rpre, s_rpost = (sem("x_squared"), sem("squares_added"), sem("sums_of_squares"),
                                                 sem("rms_pre"), sem("rms_post"))
        s_sqf = sem("square_buffer_added")
        s_yr = sem("y_normed")
        s_g, s_mid = sem("g_made"), sem("mid_split")
        s_eps, s_lbx, s_lbe = sem("eps_set"), sem("bound_logits_shifted"), sem("bound_exp")
        s_f, s_lnf, s_scan = sem("forget_gates"), sem("forget_logs"), sem("decays_summed")
        s_vcopy, s_swish = sem("v_copied"), sem("swish_split")
        s_vt, s_gate, s_gate_hi = sem("v_transposed"), sem("gated"), sem("gated_high")
        s_conv, s_lnsum, s_cent = sem("convolved"), sem("channel_sum"), sem("centred")
        s_csq, s_lnsq, s_lnr, s_lnn = sem("centred_squared"), sem("squares_summed"), sem("inverse_deviation"), sem("normed")
        s_lna, s_lns, s_lnh = sem("affine_sigmoid"), sem("swish"), sem("swish_high")
        s_dist, s_dec, s_kq, s_lv = sem("exponents"), sem("decays"), sem("decayed_kq"), sem("level_products")
        s_msum, s_pairs = sem("levels_added"), sem("pair_weights")
        s_o, s_osq, s_on, s_or = sem("head_output"), sem("head_squared"), sem("head_square_sum"), sem("head_inverse_rms")
        s_win, s_sc, s_sm, s_ex, s_p = sem("v_windows"), sem("scores"), sem("scores_shifted"), sem("exponentials"), sem("probabilities")
        s_pt, s_ptc, s_pv, s_d = sem("probabilities_transposed"), sem("probabilities_copied"), sem("weighted_v"), sem("attended")
        s_dhi, s_dlo = sem("attended_high"), sem("attended_split")
        s_c, s_chi = sem("short_convolved"), sem("short_convolved_high")

        block = ctx.enter_context(nc.Block())

        G0 = {}
        for i, (kind, j) in enumerate(IN0):
            if kind in "afg":
                G0[i] = len(G0) + 1
        N_G0 = len(G0)

        G_OUT0 = N_G0
        G_FF0 = G_OUT0 + OUT_TASKS
        G_OUT1 = G_FF0 + BLOCK * FF_BLOCKS + BLOCK
        G_FF1 = G_OUT1 + OUT_TASKS
        M_OUT0 = 0
        M_FF0 = M_OUT0 + HEADS // 2
        M_OUT1 = M_FF0 + BLOCK * FF_BLOCKS
        M_FF1 = M_OUT1 + C_TILES // 2

        def wait(eng, s, n, blk=0, per=0):
            eng.wait_ge(s, blk * per + n if per else n)

        @block.sync
        def _(sp):
            sp.dma_start(vec[:, :], vecs).then_inc(s_vec, 16)

            def piece(i, pc, first=False):
                if first:
                    src = w[i, :, pc * PW:(pc + 1) * PW]
                else:
                    sp.wait_ge(s_lo, i * PIECES + (pc + 1 - PIECES))
                    src = w[bass.ds(i, 1), :, pc * PW:(pc + 1) * PW].rearrange("a p n -> (a p) n")
                sp.dma_start(raw[:, pc * PW:(pc + 1) * PW], src).then_inc(s_raw[pc], 16)

            for pc in range(PIECES):
                piece(0, pc, first=True)
                part = slice(pc * KP * SEQ, (pc + 1) * KP * SEQ)
                sp.dma_start(x[:, part], xin[:, part]).then_inc(s_x[pc], 16)
            sp.dma_start(con[:, :], consts).then_inc(s_con, 16)
            with sp.Fori(1, TASKS) as i:
                for pc in range(PIECES):
                    piece(i, pc)
            for k in range(0, KT, 4):
                sp.wait_ge(s_xn, 3 * KT + k + 4)
                sp.dma_start(out[:, k * SEQ:(k + 4) * SEQ], tile(x, k, 4)).then_inc(s_out, 16)
            sp.wait_ge(s_out, 64)

        @block.gpsimd
        def _(pool):
            def norm(n, first=T_DVE):
                pool.wait_ge(s_rpost, n)
                for k in range(first, KT):
                    pool.tensor_tensor(tile(y, k), tile(y, k), rpost[:, :], ALU.mult).then_inc(s_yr, 1)

            pool.wait_ge(s_mid, M_OUT0 + HEADS // 2)
            pool.wait_ge(s_swish, 2)
            pool.dma_start(x[:, :], xin).then_inc(s_back, 16)
            norm(1)
            norm(2)
            pool.wait_ge(s_xsq, 3 * KT)
            pool.dma_start(xsave, x[:, :]).then_inc(s_spill, 16)
            pool.dma_start(wk[:, 0:1024], bias).then_inc(s_bias, 16)
            pool.wait_ge(s_mid, M_OUT1 + C_TILES // 2)
            pool.wait_ge(s_dlo, 1)
            pool.wait_ge(s_spill, 16)
            pool.dma_start(x[:, :], xsave).then_inc(s_back, 16)
            norm(3)
            norm(4, T_DVE_LAST)

        @block.tensor
        def _(pe):
            pe.wait_ge(s_con, 16)

            def dense(i, blk=0, per=0, moving=(in_hi, in_lo), ready=None, after=None, beside=None):
                mh, ml = moving
                for pc in range(PIECES):
                    wait(pe, s_lo, i * PIECES + pc + 1, blk, per * PIECES)
                    if pc == 0 and i >= 4:
                        wait(pe, s_taken, i - 3, blk, per)
                    for kq in range(KP):
                        k = pc * KP + kq
                        if ready:
                            ready(k)
                        for m in range(MT):
                            o = ((i % 2) * PIECES + pc) * PW + kq * COLS + m * P
                            dst = dense_bank[i % 4][:, m * SEQ:(m + 1) * SEQ]
                            wh, wl = w_hi[:, o:o + P], w_lo[:, o:o + P]
                            xh, xl = tile(mh, k), tile(ml, k)
                            pe.matmul(dst, wh, xh, start=(k == 0 and m == 0), stop=False, skip_group_check=True)
                            pe.matmul(dst, wh, xl, start=False, stop=False, skip_group_check=True)
                            mmul = pe.matmul(dst, wl, xh, start=False, stop=(k == KT - 1), skip_group_check=True)
                        if kq == KP - 1:
                            mmul.then_inc(s_mul, 1)
                        if after:
                            after(k)
                    if beside:
                        beside(pc)

            def in_ready(phase):
                return lambda k: pe.wait_ge(s_inl, phase * KT + k + 1)

            def x_squares(phase):
                def add(k):
                    pe.wait_ge(s_xsq, phase * KT + k + 1)
                    ins = pe.matmul(stat[:, 0:SEQ], ones, tile(y, k), start=(k == 0), stop=(k == KT - 1))
                    if k == KT - 1:
                        ins.then_inc(s_stat, 1)
                return add

            def norm_sum(n):
                pe.wait_ge(s_sum, n)
                pe.matmul(stat[:, 0:SEQ], ones, sqsum[:, :], start=True, stop=True).then_inc(s_stat, 1)

            def hgrn(tick):
                for j in range(HEADS // 2):
                    if tick == after_task("i", j, IN0):
                        pe.wait_ge(s_taken, IN0.index(("i", j)) + 1)
                        if j:
                            pe.wait_ge(s_or, 2 * j)
                        for m in range(MT):
                            for tt in range(2):
                                ins = pe.transpose(misc[:, (2 * m + tt) * P:(2 * m + tt + 1) * P],
                                                   tile(u, m)[:, tt * P:(tt + 1) * P], ident)
                        ins.then_inc(s_vt, 1)
                for n in range(HEADS):
                    stage = tick - HEAD_TICK[n]
                    if stage == 5:
                        pe.wait_ge(s_kq, n + 1)
                        pe.wait_ge(s_vcopy, n // 2 + 1)
                        if n:
                            pe.wait_ge(s_or, n)
                        for tt in range(2):
                            for b in range(2):
                                t0 = tt * P + b * CHUNK
                                for l in range(LEVELS):
                                    src = (tile(kk, n), tile(qq, n)) if l == 0 else (mm[l - 1], mm[l - 1])
                                    lhs, rhs = (z[:, t0:t0 + CHUNK] for z in src)
                                    pe.matmul(lev[tt][b * CHUNK:(b + 1) * CHUNK, l * CHUNK:(l + 1) * CHUNK], lhs, rhs,
                                              start=(l == 0), stop=True, skip_group_check=True)
                            pe.matmul(lev[tt][0:CHUNK, LEVELS * CHUNK:], mm[6][:, tt * P:tt * P + CHUNK],
                                      mm[6][:, tt * P + CHUNK:(tt + 1) * P], start=False, stop=True, skip_group_check=True)
                        pe.matmul(misc[:, 2 * P:3 * P], mx_cross[:, 0:P], mx_cross[:, P:2 * P], start=True,
                                  stop=True).then_inc(s_lv, 1)
                    if stage == 8:
                        pe.wait_ge(s_pairs, n + 1)
                        v0, v1 = vtok[:, n * P:(n + 1) * P], vtok[:, (HEADS + n) * P:(HEADS + n + 1) * P]
                        pe.matmul(misc[:, 0:P], v0, pairs[:, 0:P], start=True, stop=True, skip_group_check=True)
                        pe.matmul(misc[:, P:2 * P], v0, pairs[:, 2 * P:3 * P], start=False, stop=False, skip_group_check=True)
                        pe.matmul(misc[:, P:2 * P], v1, pairs[:, P:2 * P], start=False, stop=True,
                                  skip_group_check=True).then_inc(s_o, 1)
                    if stage == 9:
                        pe.wait_ge(s_osq, n + 1)
                        pe.matmul(misc[:, 2 * P:4 * P], ones, sqsum[:, :], start=True, stop=True,
                                  skip_group_check=True).then_inc(s_on, 1)

            def layernorm(tick):
                stage = tick - NORM_TICK
                if stage == 0:
                    pe.wait_ge(s_conv, A_TILES)
                    for j in range(A_TILES):
                        ins = pe.matmul(stat[:, 0:SEQ], ones, tile(conv, j), start=(j == 0), stop=(j == A_TILES - 1))
                    ins.then_inc(s_lnsum, 1)
                if stage in (3, 5):
                    h = (stage - 3) // 2
                    pe.wait_ge(s_csq, h + 1)
                    for q in range(4):
                        ins = pe.matmul(stat[:, SEQ:2 * SEQ], ones, tile(lnsq, q),
                                        start=(h == 0 and q == 0), stop=(h == 1 and q == 3))
                    ins.then_inc(s_lnsq, 1)

            def attention(tick):
                for r, t0 in enumerate(ATT_TICK):
                    stage = tick - t0
                    c, gr = r // GROUPS, r % GROUPS
                    n = CHUNK if c == 0 else WIN
                    rows = slice(gr * DH, (gr + 1) * DH)
                    if stage == 0:
                        if r == 0:
                            pe.wait_ge(s_taken, START_IN1 + IN1.index(("q", 3)) + 1)
                        k0 = max(c - 1, 0) * CHUNK
                        for jp in range(4):
                            q0 = (c * C_TILES + 2 * jp) * CHUNK
                            ins = pe.matmul(lev[0][:, jp * P:jp * P + n], qT[rows, q0:q0 + 2 * CHUNK], kT[rows, k0:k0 + n],
                                            start=(jp == 0), stop=True, skip_group_check=True)
                        ins.then_inc(s_sc, 1)
                    if stage == 3:
                        pe.wait_ge(s_p, r + 1)
                        for jp in range(4):
                            ins = pe.transpose(lev[1][0:n, jp * P:(jp + 1) * P], sc[:, jp * P:jp * P + n], ident)
                        ins.then_inc(s_pt, 1)
                    if stage == 4:
                        pe.wait_ge(s_ptc, r + 1)
                        if r:
                            pe.wait_ge(s_d, r)
                        v0 = max(c - 1, 0) * P + gr * DH
                        pe.matmul(misc[rows, :], vwin[0:n, v0:v0 + DH], pT[0:n, :], start=True, stop=True).then_inc(s_pv, 1)

            for t in range(len(IN0)):
                def beside(pc):
                    hgrn(PIECES * t + pc)
                    layernorm(PIECES * t + pc)
                dense(t, ready=in_ready(0) if t == 0 else None, after=x_squares(0) if t == 0 else None, beside=beside)

            def mid_ready(base, blk=0, per=0):
                return lambda k: wait(pe, s_mid, base + k // 2 + 1, blk, per) if k % 2 == 0 else None

            def mid_ready0(k):
                if k < A_TILES:
                    pe.wait_ge(s_swish, k // 4 + 1)
                elif k % 2 == 0:
                    pe.wait_ge(s_mid, M_OUT0 + (k - A_TILES) // 2 + 1)

            def mid_ready1(k):
                if k < C_TILES:
                    pe.wait_ge(s_mid, M_OUT1 + k // 2 + 1)
                elif k == C_TILES:
                    pe.wait_ge(s_dlo, 1)

            def out_projection(start, ready, n):
                for t in range(OUT_TASKS):
                    dense(start + t, moving=(mid_hi, mid_lo), ready=ready if t == 0 else None)
                norm_sum(n)

            def ffn(start, base, phase, n):
                dense(start, ready=in_ready(phase), after=x_squares(phase))
                for t in range(1, BLOCK):
                    dense(start + t)
                for t in range(BLOCK):
                    dense(start + BLOCK + t, moving=(mid_hi, mid_lo), ready=mid_ready(base) if t == 0 else None)
                with pe.Fori(1, FF_BLOCKS) as blk:
                    for t in range(BLOCK):
                        dense(start + t, blk, 2 * BLOCK)
                    for t in range(BLOCK):
                        dense(start + BLOCK + t, blk, 2 * BLOCK, moving=(mid_hi, mid_lo),
                              ready=mid_ready(base, blk, BLOCK) if t == 0 else None)
                norm_sum(n)

            out_projection(START_OUT0, mid_ready0, 1)
            ffn(START_FF0, M_FF0, 1, 2)

            for t in range(len(IN1)):
                def beside(pc):
                    if PIECES * t + pc == PIECES:
                        pe.wait_ge(s_taken, START_IN1 + 1)
                        for c in range(1, 4):
                            ins = pe.transpose(misc[:, (c - 1) * P:c * P], vT[:, (c - 1) * CHUNK:(c + 1) * CHUNK], ident)
                        ins.then_inc(s_win, 1)
                    attention(PIECES * t + pc)
                dense(START_IN1 + t, ready=in_ready(2) if t == 0 else None, after=x_squares(2) if t == 0 else None,
                      beside=beside)
            out_projection(START_OUT1, mid_ready1, 3)
            ffn(START_FF1, M_FF1, 3, 4)

        @block.scalar
        def _(act):
            ck = Clock(act, s_act)

            def split_piece(i, pc, blk=0, per=0):
                wait(act, s_raw[pc], 16 * (i + 1), blk, 16 * per)
                if i >= 2:
                    wait(act, s_mul, (i - 2) * PIECES + pc + 1, blk, per * PIECES)
                o = ((i % 2) * PIECES + pc) * PW
                act.activation(w_hi[:, o:o + PW], raw[:, pc * PW:(pc + 1) * PW], ACT.Copy).then_inc(s_hi, 1)

            def split(i, blk=0, per=0, between=None, beside=None):
                for pc in range(PIECES):
                    split_piece(i, pc, blk, per)
                    if pc == 1 and between:
                        between()
                    if beside:
                        beside(pc)

            def inverse_rms(n, dst, done):
                act.wait_ge(s_stat, n)
                ck.link(act.activation(dst, stat[:, 0:SEQ], ACT.Ln, scale=1.0 / D, bias=eps))
                act.activation(dst, dst, ACT.Exp, scale=-0.5).then_inc(done, 1)

            def next_input(phase):
                i = (0, START_FF0, START_IN1, START_FF1)[phase]
                for k in range(KT):
                    if phase == 0:
                        if k % KP == 0:
                            split_piece(0, k // KP)
                            act.wait_ge(s_x[k // KP], 16)
                        if k == 0:
                            act.wait_ge(s_vec, 16)
                    else:
                        act.wait_ge(s_xn, (phase - 1) * KT + k + 1)
                    act.activation(tile(in_hi, k), tile(x, k), ACT.Copy,
                                   scale=vcol(V_NORM + 2 * phase * KT + k)).then_inc(s_inh, 1)
                    act.activation(tile(y, k), tile(x, k), ACT.Square).then_inc(s_xsq, 1)
                    for pc in pieces_after(phase, k):
                        split_piece(i + 1, pc)

            def hidden(i, t, blk=0, per=0):
                wait(act, s_taken, i + 1, blk, per)
                ck.link(act.activation(g[:, :], u[:, :], ACT.Square))
                act.activation(tile(mid_hi, MT * t, MT), g[:, :], ACT.Copy).then_inc(s_g, 1)

            def squares(i, t):
                act.wait_ge(s_taken, i + 1)
                act.activation(g[:, :], tile(y, MT * t, MT), ACT.Square).then_inc(s_g, 1)

            def hgrn(tick):
                for j in range(HEADS // 2):
                    if tick == SCAN_TICK[j]:
                        act.wait_ge(s_f, j + 1)
                        act.activation(tile(bb, 2 * j, 2), tile(bb, 2 * j, 2), ACT.Ln).then_inc(s_lnf, 1)
                    if tick == after_task("i", j, IN0):
                        act.wait_ge(s_vt, j + 1)
                        for m in range(MT):
                            h0 = (2 * j + m) * P
                            ins = act.activation(v3(vtok, HEADS * P)[:, :, h0:h0 + P], v3(misc[:, m * 2 * P:(m + 1) * 2 * P], P),
                                                 ACT.Copy)
                        ins.then_inc(s_vcopy, 1)
                for n in range(HEADS):
                    stage = tick - HEAD_TICK[n]
                    b = tile(bb, n)
                    if stage == 1:
                        act.wait_ge(s_dist, n + 1)
                        six = spare[:, 0:6 * SEQ]
                        ck.link(act.activation(six, six, ACT.Abs))
                        act.activation(six, six, ACT.Exp, scale=-1.0).then_inc(s_dec, 1)
                    if stage == 2:
                        act.activation(v3(mm[6], 2 * CHUNK)[:, :, CHUNK:], v3(b, 2 * CHUNK)[:, :, CHUNK:], ACT.Exp)
                        for dst, c, scale, shift in (
                                (mm[6], 0, -1.0, b[:, CHUNK - 1:CHUNK]), (mm[6], 2, -1.0, b[:, 3 * CHUNK - 1:3 * CHUNK]),
                                (mx_cross, 0, -1.0, tail2[:, n:n + 1]), (mx_cross, 1, -1.0, b[:, 2 * CHUNK - 1:2 * CHUNK]),
                                (mx_cross, 2, 1.0, None), (mx_cross, 3, 1.0, b[:, 3 * CHUNK - 1:3 * CHUNK])):
                            part = slice(c * CHUNK, (c + 1) * CHUNK)
                            if shift is None:
                                ins = act.activation(dst[:, part], b[:, part], ACT.Exp)
                            else:
                                ins = act.activation(dst[:, part], b[:, part], ACT.Exp, scale=scale, bias=shift)
                        ins.then_inc(s_dec, 1)
                    if stage == 6:
                        act.wait_ge(s_lv, n + 1)
                        act.activation(pairs[:, 2 * P:3 * P], misc[:, 2 * P:3 * P], ACT.Copy)
                    if stage == 7:
                        act.wait_ge(s_msum, n + 1)
                        act.activation(v3(pairs[:, :], P)[0:CHUNK, 0:2, CHUNK:],
                                       v3(levels[:, :], 512)[0:CHUNK, :, LEVELS * CHUNK:], ACT.Copy)
                        for h in range(2):
                            rows = slice(h * CHUNK, (h + 1) * CHUNK)
                            ins = act.activation(v3(pairs[:, 0:2 * P], P)[rows, :, rows], v3(msum, CHUNK)[rows, :, :], ACT.Copy)
                        ins.then_inc(s_pairs, 1)
                    if stage == 8:
                        act.wait_ge(s_o, n + 1)
                        ck.link(act.activation(tile(qq, n), misc[:, 0:SEQ], ACT.Copy))
                        act.activation(sqsum[:, :], tile(qq, n), ACT.Square).then_inc(s_osq, 1)
                    if stage == 9:
                        act.wait_ge(s_on, n + 1)
                        ck.link(act.activation(sqsum[:, :], misc[:, 2 * P:4 * P], ACT.Ln, scale=1.0 / P, bias=eps))
                        act.activation(sqsum[:, :], sqsum[:, :], ACT.Exp, scale=-0.5).then_inc(s_or, 1)

            def layernorm(tick):
                stage = tick - NORM_TICK
                if stage in (2, 4):
                    h = (stage - 2) // 2
                    act.wait_ge(s_cent, 1)
                    if h:
                        act.wait_ge(s_lnsq, h)
                    act.activation(lnsq, tile(conv, 4 * h, 4), ACT.Square).then_inc(s_csq, 1)
                if stage == 6:
                    act.wait_ge(s_lnsq, 2)
                    ck.link(act.activation(acc2[:, :], stat[:, SEQ:2 * SEQ], ACT.Ln, scale=1.0 / (A_TILES * P), bias=eps))
                    act.activation(acc2[:, :], acc2[:, :], ACT.Exp, scale=-0.5).then_inc(s_lnr, 1)
                if stage == 8:
                    act.wait_ge(s_lnn, 1)
                    for j in range(A_TILES):
                        ck.mark(act.activation(tile(conv, j), tile(conv, j), ACT.Identity, scale=vcol(V_LNW + j), bias=vcol(V_LNB + j)))
                if stage in (9, 11):
                    h = (stage - 9) // 2
                    ck.settle()
                    if h:
                        act.wait_ge(s_lns, h)
                    act.activation(lnsq, tile(conv, 4 * h, 4), ACT.Sigmoid).then_inc(s_lna, 1)
                if stage == 13:
                    for h in range(2):
                        act.wait_ge(s_lns, h + 1)
                        act.activation(tile(mid_hi, 4 * h, 4), tile(conv, 4 * h, 4), ACT.Copy).then_inc(s_lnh, 1)

            def attention(tick):
                for r, t0 in enumerate(ATT_TICK):
                    stage = tick - t0
                    c, gr = r // GROUPS, r % GROUPS
                    n = CHUNK if c == 0 else WIN
                    rows = slice(gr * DH, (gr + 1) * DH)
                    if stage == 1:
                        act.wait_ge(s_sm, r + 1)
                        act.activation(esink, esink, ACT.Exp)
                        s4 = v3(sc, P)[:, :, 0:n]
                        act.activation(s4, s4, ACT.Exp).then_inc(s_ex, 1)
                    if stage == 3:
                        act.wait_ge(s_pt, r + 1)
                        act.activation(pT[0:n, :], lev[1][0:n, :], ACT.Copy).then_inc(s_ptc, 1)
                    if stage == 4:
                        act.wait_ge(s_pv, r + 1)
                        act.activation(v3(dT, SEQ)[rows, :, c * CHUNK:(c + 1) * CHUNK], v3(misc[rows, :], CHUNK),
                                       ACT.Copy).then_inc(s_d, 1)
                if tick == ATT_END:
                    act.wait_ge(s_d, len(ATT_TICK))
                    act.activation(tile(mid_hi, 8, 8), dT, ACT.Copy).then_inc(s_dhi, 1)

            act.wait_ge(s_eps, 1)
            next_input(0)

            act.wait_ge(s_lbx, 1)
            act.activation(small[:, 32:48], small[:, 32:48], ACT.Exp).then_inc(s_lbe, 1)
            def gated_high(j):
                act.wait_ge(s_gate, j + 1)
                act.activation(tile(mid_hi, 8 + 2 * j, 2), g[:, :], ACT.Copy).then_inc(s_gate_hi, 1)

            for t, (kind, j) in enumerate(IN0):
                def beside(pc):
                    hgrn(PIECES * t + pc)
                    layernorm(PIECES * t + pc)
                if t == 0:
                    inverse_rms(1, rpre[:, :], s_rpre)
                else:
                    split(t + 1, between=(lambda: gated_high(j - 1)) if kind == "g" and j else None, beside=beside)
                if kind in "afg":
                    act.wait_ge(s_taken, t + 1)
                    if kind == "a":
                        act.activation(g[:, 0:SEQ], u[:, SEQ:2 * SEQ], ACT.Sigmoid).then_inc(s_g, 1)
                    else:
                        act.activation(g[:, :], u[:, :], ACT.Sigmoid).then_inc(s_g, 1)
            gated_high(HEADS // 2 - 1)

            def out_projection(start):
                for t in range(OUT_TASKS):
                    split(start + t + 1)
                    squares(start + t, t)

            def ffn(start, n):
                per = 2 * BLOCK
                for t in range(BLOCK):
                    if t == 0:
                        inverse_rms(n, rpre[:, :], s_rpre)
                    else:
                        split(start + t + 1)
                    hidden(start + t, t)
                for t in range(BLOCK):
                    split(start + BLOCK + t + 1)
                n0 = ck.n
                with act.Fori(1, FF_BLOCKS - 1) as blk:
                    ck.rt = (blk - 1) * BLOCK
                    for t in range(BLOCK):
                        split(start + t + 1, blk, per)
                        hidden(start + t, t, blk, per)
                    for t in range(BLOCK):
                        split(start + BLOCK + t + 1, blk, per)
                assert ck.n == n0 + BLOCK
                ck.rt, ck.n = 0, n0 + BLOCK * (FF_BLOCKS - 2)
                s2 = start + per * (FF_BLOCKS - 1)
                for t in range(BLOCK):
                    split(s2 + t + 1)
                    hidden(s2 + t, t)
                for t in range(BLOCK):
                    if s2 + BLOCK + t + 1 < TASKS:
                        split(s2 + BLOCK + t + 1)
                    squares(s2 + BLOCK + t, t)

            out_projection(START_OUT0)
            inverse_rms(2, rpost[:, :], s_rpost)
            next_input(1)
            ffn(START_FF0, 3)
            inverse_rms(4, rpost[:, :], s_rpost)
            next_input(2)

            for t, (kind, j) in enumerate(IN1):
                if t == 0:
                    inverse_rms(5, rpre[:, :], s_rpre)
                else:
                    split(START_IN1 + t + 1, beside=lambda pc: attention(PIECES * t + pc))
                if kind == "c" and j % 3:
                    n = 2 * (j // 3) + (j % 3 - 1)
                    act.wait_ge(s_c, n + 1)
                    act.activation(tile(mid_hi, n), cacc, ACT.Copy).then_inc(s_chi, 1)

            out_projection(START_OUT1)
            inverse_rms(6, rpost[:, :], s_rpost)
            next_input(3)
            ffn(START_FF1, 7)
            inverse_rms(8, rpost[:, :], s_rpost)

        @block.vector
        def _(dve):
            ck = Clock(dve, s_dve)

            def split_piece(i, pc, blk=0, per=0):
                wait(dve, s_hi, i * PIECES + pc + 1, blk, per * PIECES)
                o = ((i % 2) * PIECES + pc) * PW
                dve.tensor_tensor(w_lo[:, o:o + PW], raw[:, pc * PW:(pc + 1) * PW], w_hi[:, o:o + PW],
                                  ALU.subtract).then_inc(s_lo, 1)

            def split(i, blk=0, per=0, between=None, beside=None):
                for pc in range(PIECES):
                    split_piece(i, pc, blk, per)
                    if pc == 1 and between:
                        between()
                    if beside:
                        beside(pc)

            def result(i, blk=0, per=0):
                wait(dve, s_mul, (i + 1) * PIECES, blk, per * PIECES)
                return v3(dense_bank[i % 4][:, :], SEQ)

            def scaled(dst, i):
                return dve.tensor_tensor(v3(dst, SEQ), result(i), per_token(rpre[:, :], MT), ALU.mult)

            def next_input(phase, alone=T_DVE):
                i = (0, START_FF0, START_IN1, START_FF1, 0)[phase]
                if phase == 0:
                    dve.wait_ge(s_vec, 16)
                else:
                    dve.wait_ge(s_rpost, phase)
                for k in range(KT):
                    if phase > 0:
                        if k < alone:
                            if k == 0:
                                ck.mark(dve.tensor_tensor(tile(y, k), tile(y, k), rpost[:, :], ALU.mult))
                            if k + 1 < alone:
                                ck.mark(dve.tensor_tensor(tile(y, k + 1), tile(y, k + 1), rpost[:, :], ALU.mult))
                            ck.settle(1 if k + 1 < alone else 0)
                        else:
                            dve.wait_ge(s_yr, (phase - 1) * (KT - T_DVE) + k - alone + 1)
                        dve.scalar_tensor_tensor(out=tile(x, k), in0=tile(y, k), scalar=vcol(V_NORM + (2 * phase - 1) * KT + k),
                                                 in1=tile(x, k), op0=ALU.mult, op1=ALU.add).then_inc(s_xn, 1)
                    if phase == 4:
                        continue
                    if phase == 0 and k % KP == 0:
                        split_piece(0, k // KP)
                    dve.wait_ge(s_inh, phase * KT + k + 1)
                    dve.scalar_tensor_tensor(out=tile(in_lo, k), in0=tile(x, k), scalar=vcol(V_NORM + 2 * phase * KT + k),
                                             in1=tile(in_hi, k), op0=ALU.mult, op1=ALU.subtract).then_inc(s_inl, 1)
                    for pc in pieces_after(phase, k):
                        split_piece(i + 1, pc)

            dve.memset(small[:, :], EPS).then_inc(s_eps, 1)
            ck.mark(dve.memset(hpad, 0.0))
            ck.link(dve.memset(pairs[:, :], 0.0))
            next_input(0)
            l0, l1 = vec[:, V_LB:V_LB + HEADS], vec[:, V_LB + HEADS:V_LB + 2 * HEADS]
            e0, e1, top = small[:, 32:40], small[:, 40:48], small[:, 48:56]
            ck.link(dve.tensor_tensor(top, l0, l1, ALU.max))
            ck.link(dve.tensor_tensor(e0, l0, top, ALU.subtract))
            dve.tensor_tensor(e1, l1, top, ALU.subtract).then_inc(s_lbx, 1)
            dve.wait_ge(s_lbe, 1)
            ck.link(dve.tensor_tensor(top, e0, e1, ALU.add))
            ck.link(dve.reciprocal(top, top))
            ck.link(dve.tensor_tensor(lb, e0, top, ALU.mult))
            ck.link(dve.tensor_scalar(omlb, lb, -1.0, 1.0, ALU.mult, ALU.add))

            def late0(t):
                if t < 0 or IN0[t][0] not in "afg":
                    return
                kind, j = IN0[t]
                dve.wait_ge(s_g, G0[t])
                if kind == "a":
                    o = (j % HBUF) * HP + A_CONV - 1
                    ck.link(dve.tensor_tensor(hpad[:, o:o + SEQ], u[:, 0:SEQ], g[:, 0:SEQ], ALU.mult))
                elif kind == "f":
                    for m in range(MT):
                        n = 2 * j + m
                        ck.mark(dve.tensor_scalar(tile(bb, n), tile(g, m), omlb[:, n:n + 1], lb[:, n:n + 1], ALU.mult, ALU.add))
                    ck.settle()
                    dve.tensor_scalar(tile(kk, 2 * j, 2), tile(bb, 2 * j, 2), -1.0, 1.0, ALU.mult, ALU.add).then_inc(s_f, 1)
                else:
                    ck.link(dve.tensor_tensor(g[:, :], u[:, :], g[:, :], ALU.mult))
                    dve.tensor_tensor(g[:, :], g[:, :], tile(qq, 2 * j, 2), ALU.mult).then_inc(s_gate, 1)
                    dve.wait_ge(s_gate_hi, j + 1)
                    dve.tensor_tensor(tile(mid_lo, 8 + 2 * j, 2), g[:, :], tile(mid_hi, 8 + 2 * j, 2), ALU.subtract).then_inc(s_mid, 1)

            def hgrn(tick):
                for j in range(HEADS // 2):
                    if tick == SCAN_TICK[j] + 1:
                        dve.wait_ge(s_lnf, j + 1)
                        for n in (2 * j, 2 * j + 1):
                            ck.mark(dve.tensor_tensor_scan(tile(bb, n), con[:, C_RESET:C_RESET + SEQ], tile(bb, n), 0.0,
                                                           ALU.mult, ALU.add))
                        ck.settle()
                        b3 = v3(tile(bb, 2 * j, 2), SEQ)
                        ck.link(dve.tensor_tensor(tail2[:, 2 * j:2 * j + 2].unsqueeze(2), b3[:, :, CHUNK - 1:CHUNK],
                                                  b3[:, :, 2 * CHUNK - 1:2 * CHUNK], ALU.add))
                for n in range(HEADS):
                    stage = tick - HEAD_TICK[n]
                    b, k, q = tile(bb, n), tile(kk, n), tile(qq, n)

                    def decayed(m, half):
                        m3, k3, q3 = (v3(z, 2 * half) for z in (m, k, q))
                        ck.mark(dve.tensor_tensor(m3[:, :, 0:half], m3[:, :, 0:half], k3[:, :, 0:half], ALU.mult))
                        return dve.tensor_tensor(m3[:, :, half:], m3[:, :, half:], q3[:, :, half:], ALU.mult)

                    if stage == 0:
                        for l, half in enumerate(HALVES[1:]):
                            m3, b3 = v3(mm[l], 2 * half), v3(b, 2 * half)
                            ref = b3[:, :, half - 1:half].to_broadcast([P, SEQ // (2 * half), 2 * half])
                            ins = dve.tensor_tensor(m3, b3, ref, ALU.subtract)
                            if l < 5:
                                ck.mark(ins)
                        ins.then_inc(s_dist, 1)
                    if stage == 3:
                        dve.wait_ge(s_dec, 2 * n + 1)
                        for l, half in enumerate(HALVES[1:]):
                            ck.mark(decayed(mm[l], half))
                    if stage == 4:
                        dve.wait_ge(s_dec, 2 * n + 2)
                        ck.mark(decayed(mm[6], CHUNK))
                        decayed(mx_cross, P).then_inc(s_kq, 1)
                    if stage == 6:
                        dve.wait_ge(s_lv, n + 1)
                        w1 = LEVELS * CHUNK
                        mask = con[:, C_MASK:C_MASK + w1].unsqueeze(1).to_broadcast([P, 2, w1])
                        ck.link(dve.tensor_tensor(v3(masked, w1), v3(levels[:, :], 512)[:, :, 0:w1], mask, ALU.mult))
                        dve.tensor_reduce(v3(msum, CHUNK), masked.rearrange("p (a l t) -> p a t l", a=2, l=LEVELS), AX_X,
                                          ALU.add).then_inc(s_msum, 1)
                    if stage == 10:
                        dve.wait_ge(s_or, n + 1)
                        ck.link(dve.scalar_tensor_tensor(out=q, in0=q, scalar=vcol(V_BN), in1=sqsum[:, :], op0=ALU.mult, op1=ALU.mult))

            def layernorm(tick):
                stage = tick - NORM_TICK
                c3 = v3(conv, SEQ)
                if stage == 1:
                    dve.wait_ge(s_lnsum, 1)
                    ck.link(dve.tensor_scalar(acc2[:, :], stat[:, 0:SEQ], 1.0 / (A_TILES * P), None, ALU.mult))
                    dve.tensor_tensor(c3, c3, per_token(acc2[:, :], A_TILES), ALU.subtract).then_inc(s_cent, 1)
                if stage == 7:
                    dve.wait_ge(s_lnr, 1)
                    dve.tensor_tensor(c3, c3, per_token(acc2[:, :], A_TILES), ALU.mult).then_inc(s_lnn, 1)
                if stage in (10, 12):
                    h = (stage - 10) // 2
                    dve.wait_ge(s_lna, h + 1)
                    dve.tensor_tensor(tile(conv, 4 * h, 4), tile(conv, 4 * h, 4), lnsq, ALU.mult).then_inc(s_lns, 1)
                if stage == 13:
                    for h in range(2):
                        dve.wait_ge(s_lnh, h + 1)
                        dve.tensor_tensor(tile(mid_lo, 4 * h, 4), tile(conv, 4 * h, 4), tile(mid_hi, 4 * h, 4),
                                          ALU.subtract).then_inc(s_swish, 1)

            def attention(tick):
                for r, t0 in enumerate(ATT_TICK):
                    stage = tick - t0
                    c, gr = r // GROUPS, r % GROUPS
                    n = CHUNK if c == 0 else WIN
                    s4, b4 = v3(sc, P)[:, :, 0:n], v3(wk[:, gr * 512:(gr + 1) * 512], P)[:, :, WIN - n:]
                    sink = vec[:, V_SINK + 4 * gr:V_SINK + 4 * gr + 4]

                    def per_row(a):
                        return a.unsqueeze(2).to_broadcast([P, 4, n])

                    if stage == 1:
                        if r == 0:
                            dve.wait_ge(s_bias, 16)
                        dve.wait_ge(s_sc, r + 1)
                        ck.link(dve.tensor_tensor(s4, v3(lev[0], P)[:, :, 0:n], b4, ALU.add))
                        ck.link(dve.tensor_reduce(mx, s4, AX_X, ALU.max))
                        ck.link(dve.tensor_tensor(mx, mx, sink, ALU.max))
                        ck.mark(dve.tensor_tensor(esink, sink, mx, ALU.subtract))
                        dve.tensor_tensor(s4, s4, per_row(mx), ALU.subtract).then_inc(s_sm, 1)
                    if stage == 2:
                        dve.wait_ge(s_ex, r + 1)
                        ck.link(dve.tensor_reduce(den, s4, AX_X, ALU.add))
                        ck.link(dve.tensor_tensor(den, den, esink, ALU.add))
                        ck.link(dve.reciprocal(rden, den))
                        dve.tensor_tensor(s4, s4, per_row(rden), ALU.mult).then_inc(s_p, 1)
                if tick == ATT_END + 1:
                    dve.wait_ge(s_dhi, 1)
                    dve.tensor_tensor(tile(mid_lo, 8, 8), dT, tile(mid_hi, 8, 8), ALU.subtract).then_inc(s_dlo, 1)

            def convolve(tick):
                for j in range(A_TILES):
                    part = tick - CONV_TICK[j]
                    if not 0 <= part < CONV_TICKS:
                        continue
                    h = hpad[:, (j % HBUF) * HP:(j % HBUF + 1) * HP]
                    a = tile(conv, j)
                    for q in range(TAPS * part, min(TAPS * part + TAPS, A_CONV)):
                        wq = vcol(V_DW + j * A_CONV + q)
                        dst = a if q % 2 == 0 else acc2[:, :]
                        if q == 0:
                            ck.mark(dve.tensor_scalar(dst, h[:, 0:SEQ], wq, vcol(V_DWB + j), ALU.mult, ALU.add))
                        elif q == 1:
                            if j:
                                dve.wait_ge(s_conv, j)
                            ck.mark(dve.tensor_scalar(dst, h[:, 1:1 + SEQ], wq, None, ALU.mult))
                        else:
                            ck.settle(1)
                            ck.mark(dve.scalar_tensor_tensor(out=dst, in0=h[:, q:q + SEQ], scalar=wq, in1=dst,
                                                             op0=ALU.mult, op1=ALU.add))
                    if part == CONV_TICKS - 1:
                        ck.settle()
                        dve.tensor_tensor(a, a, acc2[:, :], ALU.add).then_inc(s_conv, 1)

            for t, (kind, j) in enumerate(IN0):
                def beside(pc):
                    tick = PIECES * t + pc
                    hgrn(tick)
                    convolve(tick)
                    layernorm(tick)
                if t == 0:
                    dve.wait_ge(s_rpre, 1)
                else:
                    split(t + 1, between=lambda: late0(t - 1), beside=beside)
                if t and IN0[t - 1][0] == "i":
                    dve.wait_ge(s_vt, IN0[t - 1][1] + 1)
                dst = tile(qq, 2 * j, 2) if kind == "q" else u[:, :]
                scaled(dst, t).then_inc(s_taken, 1)
                dve.wait_ge(s_taken, t + 1)
            late0(len(IN0) - 1)

            def add_squares(ui):
                dve.wait_ge(s_g, ui + 1)
                ck.link(dve.tensor_tensor(sqsum[:, :], sqsum[:, :], g[:, 0:SEQ], ALU.add))
                ins = dve.tensor_tensor(sqsum[:, :], sqsum[:, :], g[:, SEQ:2 * SEQ], ALU.add)
                return ins

            def finish_squares(ui):
                add_squares(ui).then_inc(s_sum, 1)

            def out_projection(start, gi):
                ck.link(dve.memset(sqsum[:, :], 0.0))
                for t in range(OUT_TASKS):
                    split(start + t + 1, between=(lambda: ck.link(add_squares(gi + t - 1))) if t else None)
                    dve.tensor_copy(v3(tile(y, MT * t, MT), SEQ), result(start + t)).then_inc(s_taken, 1)
                finish_squares(gi + OUT_TASKS - 1)

            def up(i, blk=0, per=0):
                dve.scalar_tensor_tensor(out=v3(u[:, :], SEQ), in0=result(i, blk, per), scalar=0.0,
                                         in1=per_token(rpre[:, :], MT), op0=ALU.max, op1=ALU.mult).then_inc(s_taken, 1)

            def low_hidden(gi, t, blk=0, per=0):
                wait(dve, s_g, gi + 1, blk, per)
                dve.tensor_tensor(tile(mid_lo, MT * t, MT), g[:, :], tile(mid_hi, MT * t, MT), ALU.subtract).then_inc(s_mid, 1)

            def down(i, t, first=False, blk=0, per=0):
                r = result(i, blk, per)
                dst = v3(tile(y, MT * t, MT), SEQ)
                ins = dve.tensor_copy(dst, r) if first else dve.tensor_tensor(dst, r, dst, ALU.add)
                ins.then_inc(s_taken, 1)

            def ffn(start, gi, n):
                per = 2 * BLOCK

                def ups(s0, g0, blk=0):
                    p, q = (per, BLOCK) if not isinstance(blk, int) else (0, 0)
                    for t in range(BLOCK):
                        if s0 == start and t == 0 and p == 0:
                            dve.wait_ge(s_rpre, n)
                        else:
                            split(s0 + t + 1, blk, p, between=(lambda: low_hidden(g0 + t - 1, t - 1, blk, q)) if t else None)
                        up(s0 + t, blk, p)
                    return lambda: low_hidden(g0 + BLOCK - 1, BLOCK - 1, blk, q)

                left = ups(start, gi)
                for t in range(BLOCK):
                    split(start + BLOCK + t + 1, between=left if t == 0 else None)
                    down(start + BLOCK + t, t, first=True)
                with dve.Fori(1, FF_BLOCKS - 1) as blk:
                    left = ups(start, gi, blk)
                    for t in range(BLOCK):
                        split(start + BLOCK + t + 1, blk, per, between=left if t == 0 else None)
                        down(start + BLOCK + t, t, blk=blk, per=per)
                s2, g2 = start + per * (FF_BLOCKS - 1), gi + BLOCK * (FF_BLOCKS - 1)
                left = ups(s2, g2)
                ck.link(dve.memset(sqsum[:, :], 0.0))
                for t in range(BLOCK):
                    i = s2 + BLOCK + t
                    between = left if t == 0 else (lambda: ck.link(add_squares(g2 + BLOCK + t - 1)))
                    if i + 1 < TASKS:
                        split(i + 1, between=between)
                    else:
                        between()
                    down(i, t)
                finish_squares(g2 + 2 * BLOCK - 1)

            out_projection(START_OUT0, G_OUT0)
            dve.wait_ge(s_back, 16)
            next_input(1)
            ffn(START_FF0, G_FF0, 2)
            next_input(2)

            def c_low(t):
                kind, j = IN1[t]
                if kind == "c" and j % 3:
                    n = 2 * (j // 3) + (j % 3 - 1)
                    dve.wait_ge(s_chi, n + 1)
                    ins = dve.tensor_tensor(tile(mid_lo, n), cacc, tile(mid_hi, n), ALU.subtract)
                    if n % 2:
                        ins.then_inc(s_mid, 1)
                    else:
                        ck.link(ins)

            for t, (kind, j) in enumerate(IN1):
                i = START_IN1 + t

                def beside(pc):
                    tick = PIECES * t + pc
                    if tick == PIECES + 1:
                        dve.wait_ge(s_win, 1)
                        ck.mark(dve.tensor_copy(vwin, misc[:, 0:3 * P]))
                        ck.link(dve.memset(cpad, 0.0))
                    attention(tick)
                if t == 0:
                    dve.wait_ge(s_rpre, 3)
                    dve.wait_ge(s_spill, 16)
                else:
                    split(i + 1, between=lambda: c_low(t - 1), beside=beside)
                if kind == "kv":
                    scaled(x[:, 0:512], i).then_inc(s_taken, 1)
                elif kind == "q":
                    r = result(i)
                    for m in range(MT):
                        dst = v3(qT, C_TILES * CHUNK)[:, :, (2 * j + m) * CHUNK:(2 * j + m + 1) * CHUNK]
                        ins = dve.scalar_tensor_tensor(out=dst, in0=v3(r[:, m, :], CHUNK), scalar=DH ** -0.5,
                                                       in1=v3(rpre[:, :], CHUNK), op0=ALU.mult, op1=ALU.mult)
                    ins.then_inc(s_taken, 1)
                else:
                    scaled(tile(cbuf, 2 * (j % 3), 2), i).then_inc(s_taken, 1)
                dve.wait_ge(s_taken, i + 1)
                if kind == "c" and j % 3:
                    n = 2 * (j // 3) + (j % 3 - 1)
                    hh, cc, gb = ((0, 1, 2), (3, 4, 5))[j % 3 - 1]
                    ck.link(dve.tensor_tensor(cpad[:, 2:2 + SEQ], tile(cbuf, hh), tile(cbuf, cc), ALU.mult))
                    for q in range(C_CONV):
                        wq = vcol(V_CC + n * C_CONV + q)
                        if q == 0:
                            ck.link(dve.tensor_scalar(cacc, cpad[:, 0:SEQ], wq, None, ALU.mult))
                        else:
                            ck.link(dve.scalar_tensor_tensor(out=cacc, in0=cpad[:, q:q + SEQ], scalar=wq, in1=cacc,
                                                             op0=ALU.mult, op1=ALU.add))
                    dve.tensor_tensor(cacc, cacc, tile(cbuf, gb), ALU.mult).then_inc(s_c, 1)
            c_low(len(IN1) - 1)

            out_projection(START_OUT1, G_OUT1)
            dve.wait_ge(s_back, 32)
            next_input(3)
            ffn(START_FF1, G_FF1, 4)
            next_input(4, T_DVE_LAST)


def _tiles(v):
    v = np.asarray(v)
    return v.reshape(v.shape[:-1] + (v.shape[-1] // P, P))


def _columns():
    r = np.arange(P)
    aw, hw = A_TILES * P, HEADS * P
    base = {"f": 2 * aw + hw, "q": 2 * aw, "i": 2 * aw + 2 * hw, "g": 2 * aw + 3 * hw}
    in0 = []
    for kind, j in IN0:
        if kind == "a":
            in0.append(np.concatenate([j * P + r, aw + j * P + r]))
        else:
            in0.append(base[kind] + 2 * j * P + np.arange(2 * P))
    cw = C_TILES * P
    qb, kb = 3 * cw, 3 * cw + Q_HEADS * DH
    in1 = []
    d = np.arange(DH)
    order = []
    for j in range(C_TILES // 2):
        order += [(0, 2 * j), (2, 2 * j), (1, 2 * j), (0, 2 * j + 1), (2, 2 * j + 1), (1, 2 * j + 1)]
    for kind, j in IN1:
        if kind == "kv":
            in1.append(kb + np.arange(2 * P))
        elif kind == "q":
            in1.append(np.concatenate([qb + h * DH + d for n in (2 * j, 2 * j + 1) for h in (n, Q_HEADS // 2 + n)]))
        else:
            in1.append(np.concatenate([part * cw + n * P + r for part, n in order[2 * j:2 * j + 2]]))
    return np.concatenate(in0), np.concatenate(in1)


def _head_rows():
    d = np.arange(DH)
    return np.concatenate([h * DH + d for n in range(Q_HEADS // 2) for h in (n, Q_HEADS // 2 + n)])


def _stream(parts):
    out = np.empty((TASKS, P, KT, COLS), np.float32)
    at = 0
    for m in parts:
        n = m.shape[1] // COLS
        out[at:at + n] = m.reshape(KT, P, n, COLS).transpose(2, 1, 0, 3)
        at += n
    assert at == TASKS
    return out.reshape(TASKS, P, KT * COLS)


def _constants():
    con = np.zeros((P, C_N), np.float32)
    con[:, C_ID:C_ID + P] = np.eye(P)
    con[:, C_ONE:C_ONE + P] = 1
    s, t = np.arange(P)[:, None] % CHUNK, np.arange(CHUNK)[None, :]
    for l, half in enumerate(HALVES):
        if half == 0:
            m = s == t
        else:
            m = (s // (2 * half) == t // (2 * half)) & (s % (2 * half) < half) & (t % (2 * half) >= half)
        con[:, C_MASK + l * CHUNK:C_MASK + (l + 1) * CHUNK] = m
    con[:, C_RESET:C_RESET + SEQ] = (np.arange(SEQ) % CHUNK != 0)
    slopes = (2.0 ** (-8.0 * np.arange(1, Q_HEADS + 1, dtype=np.float32) / Q_HEADS)).astype(np.float32)
    dist = np.abs(np.arange(CHUNK)[:, None] + CHUNK - np.arange(WIN)[None, :]).astype(np.float32)
    bias = np.zeros((2, CHUNK, GROUPS, 4, WIN), np.float32)
    for gr in range(GROUPS):
        for jp in range(4):
            for e in range(2):
                bias[e, :, gr, jp, :] = -slopes[8 * gr + 2 * jp + e] * dist
    return con, bias.reshape(P, GROUPS * 4 * WIN)


def kernel(x, w_in_even, w_out_even, a_dw_w, a_dw_b, a_ln_w, a_ln_b, b_lb_logits, b_norm_w, w_in_odd, w_out_odd,
           c_conv_w, d_sinks, norm_pre_mix, norm_post_mix, norm_pre_ffn, norm_post_ffn, w_ffn_up, w_ffn_down):
    import concourse.bacc as bacc
    from concourse.bass_utils import run_bass_kernel_spmd

    cols0, cols1 = _columns()
    rows1 = np.concatenate([np.arange(C_TILES * P), C_TILES * P + _head_rows()])

    def ffn(l):
        up, down = np.asarray(w_ffn_up)[l], np.asarray(w_ffn_down)[l]
        return [m for b in range(FF_BLOCKS) for m in (up[:, b * D:(b + 1) * D], down[b * D:(b + 1) * D])]

    stream = _stream([np.asarray(w_in_even)[0][:, cols0], np.asarray(w_out_even)[0], *ffn(0),
                      np.asarray(w_in_odd)[0][:, cols1], np.asarray(w_out_odd)[0][rows1], *ffn(1)])
    vec = np.empty((P, V_N), np.float32)
    norms = [np.asarray(v)[l] for l in range(2) for v in (norm_pre_mix, norm_post_mix, norm_pre_ffn, norm_post_ffn)]
    for n, v in enumerate(norms):
        vec[:, V_NORM + n * KT:V_NORM + (n + 1) * KT] = _tiles(v).T
    vec[:, V_DW:V_DWB] = _tiles(a_dw_w[0]).transpose(2, 1, 0).reshape(P, A_TILES * A_CONV)
    vec[:, V_DWB:V_LNW] = _tiles(a_dw_b[0]).T
    vec[:, V_LNW:V_LNB] = _tiles(a_ln_w[0]).T
    vec[:, V_LNB:V_LB] = _tiles(a_ln_b[0]).T
    vec[:, V_LB:V_BN] = _tiles(b_lb_logits).transpose(2, 0, 1).reshape(P, 2 * HEADS)
    vec[:, V_BN] = np.asarray(b_norm_w)[0]
    vec[:, V_CC:V_SINK] = _tiles(c_conv_w[0]).transpose(2, 1, 0).reshape(P, C_TILES * C_CONV)
    sinks = np.asarray(d_sinks)[0].reshape(GROUPS, 4, 2)
    vec[:, V_SINK:] = np.repeat(sinks.transpose(2, 0, 1).reshape(2, 1, 8), CHUNK, axis=1).reshape(P, 8)
    con, bias = _constants()
    xt = np.ascontiguousarray(np.asarray(x)[0].T.reshape(KT, P, SEQ).transpose(1, 0, 2)).reshape(P, KT * SEQ)

    arrays = {"weights": stream, "x_in": xt, "vectors": vec, "constants": con, "alibi": bias}
    nc = bacc.Bacc("TRN2", target_bir_lowering=False, num_devices=1)
    ins = [nc.dram_tensor(k, a.shape, F32, kind="ExternalInput").ap() for k, a in arrays.items()]
    xsave = nc.dram_tensor("x_save", (P, KT * SEQ), F32, kind="Internal").ap()
    out = nc.dram_tensor("out", (P, KT * SEQ), F32, kind="ExternalOutput").ap()
    bass_hybrid_trunk(nc, *ins, xsave, out)
    r = run_bass_kernel_spmd(nc, [arrays], core_ids=[0])
    got = r.results[0]["out"]
    return np.ascontiguousarray(got.reshape(P, KT, SEQ).transpose(2, 1, 0)).reshape(1, SEQ, D)
```

```python
from contextlib import ExitStack

import numpy as np

import concourse.bass as bass
from concourse import mybir

F32 = mybir.dt.float32
F32R = mybir.dt.float32r
ALU = mybir.AluOpType
ACT = mybir.ActivationFunctionType
AX_X = mybir.AxisListType.X

P = 128
SEQ = 256
D = 2048
KT = D // P
FF = 4 * D
COLS = 256
MT = COLS // P
PIECES = 4
KP = KT // PIECES
PW = KP * COLS
EPS = 1e-6

A_TILES = 8
A_CONV = 31
HEADS = 8
CHUNK = 64
C_TILES = 8
C_CONV = 3
Q_HEADS, GROUPS, DH = 16, 2, 64
WIN = 128

IN0 = [x for n in range(4) for x in (("a", 2 * n), ("f", n), ("q", n), ("a", 2 * n + 1), ("i", n))] + \
      [("g", n) for n in range(4)]
IN1 = [("kv", 0)] + [("q", j) for j in range(4)] + [("c", j) for j in range(12)]
OUT_TASKS = D // COLS
BLOCK = D // COLS
FF_BLOCKS = FF // D
START_IN0 = 0
START_OUT0 = START_IN0 + len(IN0)
START_FF0 = START_OUT0 + OUT_TASKS
START_IN1 = START_FF0 + 2 * BLOCK * FF_BLOCKS
START_OUT1 = START_IN1 + len(IN1)
START_FF1 = START_OUT1 + OUT_TASKS
TASKS = START_FF1 + 2 * BLOCK * FF_BLOCKS

V_NORM = 0
V_DW = V_NORM + 8 * KT
V_DWB = V_DW + A_TILES * A_CONV
V_LNW = V_DWB + A_TILES
V_LNB = V_LNW + A_TILES
V_LB = V_LNB + A_TILES
V_BN = V_LB + 2 * HEADS
V_CC = V_BN + 1
V_SINK = V_CC + C_TILES * C_CONV
V_N = V_SINK + Q_HEADS // 2
T_DVE, T_DVE_LAST = 4, 8


def pieces_after(phase, k):
    return ({KT - 1: (0, 1, 2, 3)} if phase == 0 else {7: (0, 1), KT - 1: (2, 3)}).get(k, ())


LEAD = 2
HBUF = 4

def after_task(kind, j, tasks):
    return PIECES * (tasks.index((kind, j)) + 1)


HEAD_GAP = 10
HEAD_TICK = [after_task("q", n // 2, IN0) + HEAD_GAP * (n % 2) for n in range(HEADS)]
SCAN_TICK = [after_task("f", j, IN0) + 3 for j in range(HEADS // 2)]
HEAD_LOAD = {0: 2, 1: 3, 3: 3, 4: 4, 5: 3, 8: 2, 9: 1, 13: 1}
TICK_LOAD = 6


def conv_taps():
    left = [(j, q) for j in range(A_TILES) for q in range(A_CONV)]
    ticks, tick = {}, 0
    while left:
        room = TICK_LOAD - sum(HEAD_LOAD.get(tick - t0, 0) for t0 in HEAD_TICK)
        while room > 0 and left and tick >= after_task("a", left[0][0], IN0) + 2:
            ticks.setdefault(tick, []).append(left.pop(0))
            room -= 1
        tick += 1
    return ticks, tick


CONV_TAPS, NORM_TICK = conv_taps()
assert max(NORM_TICK + 9, HEAD_TICK[-1] + 13) < PIECES * len(IN0)
ATT_TICK = [after_task("q", 3, IN1) + 1 + 5 * r for r in range(GROUPS * SEQ // CHUNK)]
ATT_END = ATT_TICK[-1] + 8

MID_CONV, MID_SHORT = HEADS - 2, 8


def mid_head(n):
    return n if n < MID_CONV else A_TILES + n


HALVES = [0, 1, 2, 4, 8, 16, 32]
FAR = 256
SUB = 32
LEVELS = len(HALVES) - 1
C_ID = 0
C_ONE = C_ID + P
C_MASK = C_ONE + P
C_RESET = C_MASK + LEVELS * SUB
C_N = C_RESET + SEQ



class Clock:

    def __init__(self, eng, sem):
        self.eng, self.sem, self.n, self.rt = eng, sem, 0, 0

    def mark(self, ins):
        self.n += 1
        ins.then_inc(self.sem, 1)

    def settle(self, back=0):
        if self.n > back:
            self.eng.wait_ge(self.sem, self.rt + (self.n - back))

    def link(self, ins):
        self.mark(ins)
        self.settle()


def bass_hybrid_trunk(nc: bass.Bass, w, xin, vecs, consts, bias, xsave, out):
    with ExitStack() as ctx:
        def sb(name, cols, dt=F32):
            return ctx.enter_context(nc.sbuf_tensor(name, [P, cols], dt))

        def sem(name):
            return ctx.enter_context(nc.semaphore(name))

        raw = sb("raw", PIECES * PW)
        w_hi = sb("w_hi", 2 * PIECES * PW, F32R)
        w_lo = sb("w_lo", 2 * PIECES * PW, F32R)
        in_hi = sb("in_hi", KT * SEQ, F32R)
        in_lo = sb("in_lo", KT * SEQ, F32R)
        mid_at = -(-nc.sbuf_base // 32) * 32
        spare = sb("spare", 2 * KT * SEQ)
        assert nc.sbuf_base == mid_at + 4 * 2 * KT * SEQ
        mid_hi = nc.alloc_sbuf_tensor_at("mid_hi", [P, KT * SEQ], F32R, offset=mid_at)
        mid_lo = nc.alloc_sbuf_tensor_at("mid_lo", [P, KT * SEQ], F32R, offset=mid_at + 4 * KT * SEQ)
        x = sb("x", KT * SEQ)
        y = sb("y", KT * SEQ)
        vec = sb("vec", V_N)
        con = sb("con", C_N)
        rpre = sb("rpre", SEQ)
        rpost = sb("rpost", SEQ)
        sqsum = sb("sqsum", SEQ)
        u = sb("u", MT * SEQ)
        g = sb("g", MT * SEQ)
        wk = sb("wk", 3072)
        acc2 = sb("acc2", SEQ)
        pairs = sb("pairs", 3 * P)
        small = sb("small", 64)

        dense_bank = [ctx.enter_context(nc.psum_tensor(f"dense{n}", [P, 512], F32)) for n in range(4)]
        stat, misc = (ctx.enter_context(nc.psum_tensor(n, [P, 512], F32)) for n in ("stat", "misc"))
        levels = ctx.enter_context(nc.psum_tensor("levels", [P, 1024], F32))
        lev = [levels[:, 0:512], levels[:, 512:1024]]

        ident = con[:, C_ID:C_ID + P]
        ones = con[:, C_ONE:C_ONE + P]
        eps = small[:, 0:1]
        lb, omlb = small[:, 8:16], small[:, 16:24]
        nomlb = small[:, 56:64]
        tail2 = small[:, 24:32]
        mx, esink, den, rden = small[:, 32:36], small[:, 36:40], small[:, 40:44], small[:, 44:48]

        conv, kk = x[:, 0:2048], x[:, 2048:4096]
        bb, qq = y[:, 0:2048], y[:, 2048:4096]
        vtok, lnsq = wk[:, 0:2048], wk[:, 2048:3072]
        first = MID_CONV * SEQ
        mm_all = spare[:, first:first + 7 * SEQ]
        mm = [mm_all[:, l * SEQ:(l + 1) * SEQ] for l in range(7)]
        mx_cross = spare[:, first + 7 * SEQ:first + 8 * SEQ]
        rest = first + KT * SEQ
        HP = SEQ + A_CONV - 1
        hpad = spare[:, rest + 1024:rest + 1024 + HBUF * HP]
        masked, msum = spare[:, rest:rest + 2 * LEVELS * SUB], spare[:, rest + 512:rest + 512 + 2 * SUB]
        kT, vT, vwin = x[:, 0:256], x[:, 256:512], x[:, 512:896]
        sc, pT = x[:, 896:1408], x[:, 1408:1920]
        cbuf, cpad, cacc = x[:, 1920:3456], x[:, 3456:3456 + SEQ + 2], x[:, 3714:3970]
        qT, dT = y[:, 0:2048], y[:, 2048:4096]

        def v3(ap, c):
            return ap.rearrange("p (a b) -> p a b", b=c)

        def per_token(ap, n):
            return ap.unsqueeze(1).to_broadcast([P, n, SEQ])

        def tile(ap, k, n=1):
            return ap[:, k * SEQ:(k + n) * SEQ]

        def vcol(c):
            return vec[:, c:c + 1]

        s_vec, s_con, s_bias = sem("vectors_landed"), sem("constants_landed"), sem("bias_landed")
        s_back, s_spill, s_out = sem("x_back"), sem("x_spilled"), sem("out_written")
        s_x = [sem(f"x{n}_landed") for n in range(PIECES)]
        s_raw = [sem(f"piece{n}_landed") for n in range(PIECES)]
        s_hi, s_lo, s_mul = sem("weights_high"), sem("weights_split"), sem("pieces_multiplied")
        s_taken = sem("results_taken")
        s_act, s_dve = sem("act_clock"), sem("dve_clock")
        s_xn, s_inh, s_inl = sem("x_updated"), sem("input_high"), sem("input_split")
        s_xsq, s_sum, s_stat, s_rpre, s_rpost = (sem("x_squared"), sem("squares_added"), sem("sums_of_squares"),
                                                 sem("rms_pre"), sem("rms_post"))
        s_yr = sem("y_normed")
        s_g, s_mid = sem("g_made"), sem("mid_split")
        s_eps, s_lbx, s_lbe = sem("eps_set"), sem("bound_logits_shifted"), sem("bound_exp")
        s_bound, s_lnf = sem("bounds_made"), sem("forget_logs")
        s_vcopy, s_swish = sem("v_copied"), sem("swish_split")
        s_vt, s_gate, s_gate_hi = sem("v_transposed"), sem("gated"), sem("gated_high")
        s_conv, s_lnsum, s_cent = sem("convolved"), sem("channel_sum"), sem("centred")
        s_csq, s_lnsq, s_lnr, s_lnn = sem("centred_squared"), sem("squares_summed"), sem("inverse_deviation"), sem("normed")
        s_lna, s_lns, s_lnh = sem("affine_sigmoid"), sem("swish"), sem("swish_high")
        s_dist, s_dec, s_kq, s_lv = sem("exponents"), sem("decays"), sem("decayed_kq"), sem("level_products")
        s_msum, s_pairs = sem("levels_added"), sem("pair_weights")
        s_o, s_osq, s_on, s_or = sem("head_output"), sem("head_squared"), sem("head_square_sum"), sem("head_inverse_rms")
        s_win, s_sc, s_sm, s_ex, s_p = sem("v_windows"), sem("scores"), sem("scores_shifted"), sem("exponentials"), sem("probabilities")
        s_pt, s_ptc, s_pv, s_d = sem("probabilities_transposed"), sem("probabilities_copied"), sem("weighted_v"), sem("attended")
        s_dhi, s_dlo = sem("attended_high"), sem("attended_split")
        s_c, s_chi = sem("short_convolved"), sem("short_convolved_high")

        block = ctx.enter_context(nc.Block())

        G0 = {}
        for i, (kind, j) in enumerate(IN0):
            if kind in "afg":
                G0[i] = len(G0) + 1
        N_G0 = len(G0)

        G_OUT0 = N_G0
        G_FF0 = G_OUT0 + OUT_TASKS
        G_OUT1 = G_FF0 + BLOCK * FF_BLOCKS + BLOCK
        G_FF1 = G_OUT1 + OUT_TASKS
        M_OUT0 = 0
        M_FF0 = M_OUT0 + HEADS // 2
        M_OUT1 = M_FF0 + BLOCK * FF_BLOCKS
        M_FF1 = M_OUT1 + C_TILES // 2

        def wait(eng, s, n, blk=0, per=0):
            eng.wait_ge(s, blk * per + n if per else n)

        @block.sync
        def _(sp):
            sp.dma_start(vec[:, :], vecs).then_inc(s_vec, 16)

            def piece(i, pc, first=False):
                if first:
                    src = w[i, :, pc * PW:(pc + 1) * PW]
                else:
                    sp.wait_ge(s_lo, i * PIECES + (pc + 1 - PIECES))
                    src = w[bass.ds(i, 1), :, pc * PW:(pc + 1) * PW].rearrange("a p n -> (a p) n")
                sp.dma_start(raw[:, pc * PW:(pc + 1) * PW], src).then_inc(s_raw[pc], 16)

            for pc in range(PIECES):
                piece(0, pc, first=True)
                part = slice(pc * KP * SEQ, (pc + 1) * KP * SEQ)
                sp.dma_start(x[:, part], xin[:, part]).then_inc(s_x[pc], 16)
            sp.dma_start(con[:, :], consts).then_inc(s_con, 16)
            with sp.Fori(1, TASKS) as i:
                for pc in range(PIECES):
                    piece(i, pc)
            for k in range(0, KT, 4):
                sp.wait_ge(s_xn, 3 * KT + k + 4)
                sp.dma_start(out[:, k * SEQ:(k + 4) * SEQ], tile(x, k, 4)).then_inc(s_out, 16)
            sp.wait_ge(s_out, 64)

        @block.gpsimd
        def _(pool):
            def norm(n, first=T_DVE):
                pool.wait_ge(s_rpost, n)
                for k in range(first, KT):
                    pool.tensor_tensor(tile(y, k), tile(y, k), rpost[:, :], ALU.mult).then_inc(s_yr, 1)

            pool.wait_ge(s_mid, M_OUT0 + HEADS // 2)
            pool.wait_ge(s_swish, 2)
            pool.dma_start(x[:, :], xin).then_inc(s_back, 16)
            norm(1)
            norm(2)
            pool.wait_ge(s_xsq, 3 * KT)
            pool.dma_start(xsave, x[:, :]).then_inc(s_spill, 16)
            pool.dma_start(wk[:, 0:1024], bias).then_inc(s_bias, 16)
            pool.wait_ge(s_mid, M_OUT1 + C_TILES // 2)
            pool.wait_ge(s_dlo, 1)
            pool.wait_ge(s_spill, 16)
            pool.dma_start(x[:, :], xsave).then_inc(s_back, 16)
            norm(3)
            norm(4, T_DVE_LAST)

        @block.tensor
        def _(pe):
            def dense(i, blk=0, per=0, moving=(in_hi, in_lo), ready=None, after=None, beside=None):
                mh, ml = moving
                for pc in range(PIECES):
                    wait(pe, s_lo, i * PIECES + pc + 1, blk, per * PIECES)
                    if pc == 0 and i >= 4:
                        wait(pe, s_taken, i - 3, blk, per)
                    for kq in range(KP):
                        k = pc * KP + kq
                        if ready:
                            ready(k)
                        for m in range(MT):
                            o = ((i % 2) * PIECES + pc) * PW + kq * COLS + m * P
                            dst = dense_bank[i % 4][:, m * SEQ:(m + 1) * SEQ]
                            wh, wl = w_hi[:, o:o + P], w_lo[:, o:o + P]
                            xh, xl = tile(mh, k), tile(ml, k)
                            pe.matmul(dst, wh, xh, start=(k == 0 and m == 0), stop=False, skip_group_check=True)
                            pe.matmul(dst, wh, xl, start=False, stop=False, skip_group_check=True)
                            mmul = pe.matmul(dst, wl, xh, start=False, stop=(k == KT - 1), skip_group_check=True)
                        if kq == KP - 1:
                            mmul.then_inc(s_mul, 1)
                        if after:
                            after(k)
                    if beside:
                        beside(pc)

            def in_ready(phase):
                return lambda k: pe.wait_ge(s_inl, phase * KT + k + 1)

            def x_squares(phase):
                def add(k):
                    pe.wait_ge(s_xsq, phase * KT + k + 1)
                    ins = pe.matmul(stat[:, 0:SEQ], ones, tile(y, k), start=(k == 0), stop=(k == KT - 1))
                    if k == KT - 1:
                        ins.then_inc(s_stat, 1)

                def add_all(k):
                    if k == KT - 1:
                        pe.wait_ge(s_con, 16)
                        for q in range(KT):
                            add(q)
                return add if phase else add_all

            def norm_sum(n):
                pe.wait_ge(s_sum, n)
                pe.matmul(stat[:, 0:SEQ], ones, sqsum[:, :], start=True, stop=True).then_inc(s_stat, 1)

            def hgrn(tick):
                for j in range(HEADS // 2):
                    if tick == after_task("i", j, IN0) + 1:
                        pe.wait_ge(s_taken, IN0.index(("i", j)) + 1)
                        pe.wait_ge(s_rpre, 1)
                        if j:
                            pe.wait_ge(s_vcopy, j)
                        for m in range(MT):
                            for tt in range(2):
                                ins = pe.transpose(stat[:, (2 * m + tt) * P:(2 * m + tt + 1) * P],
                                                   tile(u, m)[:, tt * P:(tt + 1) * P], ident)
                        ins.then_inc(s_vt, 1)
                for n in range(HEADS):
                    stage = tick - HEAD_TICK[n]
                    if stage == 7:
                        pe.wait_ge(s_kq, n + 1)
                        if n:
                            pe.wait_ge(s_or, n)
                        for tt in range(2):
                            for b in range(P // SUB):
                                t0 = tt * P + b * SUB
                                for l in range(LEVELS):
                                    src = ((tile(kk, n), tile(qq, n)), (tile(kk, n), mm[0]))[l] if l < 2 else (mm[l - 1], mm[l - 1])
                                    lhs, rhs = (z[:, t0:t0 + SUB] for z in src)
                                    pe.matmul(lev[tt][b * SUB:(b + 1) * SUB, l * SUB:(l + 1) * SUB], lhs, rhs,
                                              start=(l == 0), stop=True, skip_group_check=True)
                            for m, half in ((mm[5], SUB), (mm[6], CHUNK)):
                                for b in range(0, P, 2 * half):
                                    t0 = tt * P + b
                                    pe.matmul(lev[tt][b:b + half, FAR + b + half:FAR + b + 2 * half], m[:, t0:t0 + half],
                                              m[:, t0 + half:t0 + 2 * half], start=False, stop=True, skip_group_check=True)
                        pe.matmul(misc[:, 2 * P:3 * P], mx_cross[:, 0:P], mx_cross[:, P:2 * P], start=True,
                                  stop=True).then_inc(s_lv, 1)
                    if stage == 11:
                        pe.wait_ge(s_pairs, n + 1)
                        pe.wait_ge(s_vcopy, n // 2 + 1)
                        v0, v1 = vtok[:, n * P:(n + 1) * P], vtok[:, (HEADS + n) * P:(HEADS + n + 1) * P]
                        pe.matmul(misc[:, 0:P], v0, pairs[:, 0:P], start=True, stop=True, skip_group_check=True)
                        pe.matmul(misc[:, P:2 * P], v0, pairs[:, 2 * P:3 * P], start=False, stop=False, skip_group_check=True)
                        pe.matmul(misc[:, P:2 * P], v1, pairs[:, P:2 * P], start=False, stop=True,
                                  skip_group_check=True).then_inc(s_o, 1)
                    if stage == 12:
                        pe.wait_ge(s_osq, n + 1)
                        pe.matmul(misc[:, 2 * P:4 * P], ones, sqsum[:, :], start=True, stop=True,
                                  skip_group_check=True).then_inc(s_on, 1)

            def layernorm(tick):
                stage = tick - NORM_TICK
                if stage == 0:
                    pe.wait_ge(s_conv, A_TILES)
                    pe.wait_ge(s_vcopy, HEADS // 2)
                    for j in range(A_TILES):
                        ins = pe.matmul(stat[:, 0:SEQ], ones, tile(conv, j), start=(j == 0), stop=(j == A_TILES - 1))
                    ins.then_inc(s_lnsum, 1)
                if stage in (3, 4):
                    h = stage - 3
                    pe.wait_ge(s_csq, h + 1)
                    for q in range(4):
                        ins = pe.matmul(stat[:, SEQ:2 * SEQ], ones, tile(lnsq, q),
                                        start=(h == 0 and q == 0), stop=(h == 1 and q == 3))
                    ins.then_inc(s_lnsq, 1)

            def attention(tick):
                for r, t0 in enumerate(ATT_TICK):
                    stage = tick - t0
                    c, gr = r // GROUPS, r % GROUPS
                    n = CHUNK if c == 0 else WIN
                    rows = slice(gr * DH, (gr + 1) * DH)
                    if stage == 0:
                        if r == 0:
                            pe.wait_ge(s_taken, START_IN1 + IN1.index(("q", 3)) + 1)
                        k0 = max(c - 1, 0) * CHUNK
                        for jp in range(4):
                            q0 = (c * C_TILES + 2 * jp) * CHUNK
                            ins = pe.matmul(lev[0][:, jp * P:jp * P + n], qT[rows, q0:q0 + 2 * CHUNK], kT[rows, k0:k0 + n],
                                            start=(jp == 0), stop=True, skip_group_check=True)
                        ins.then_inc(s_sc, 1)
                    if stage == 4:
                        pe.wait_ge(s_p, r + 1)
                        for jp in range(4):
                            ins = pe.transpose(lev[1][0:n, jp * P:(jp + 1) * P], sc[:, jp * P:jp * P + n], ident)
                        ins.then_inc(s_pt, 1)
                    if stage == 6:
                        pe.wait_ge(s_ptc, r + 1)
                        if r:
                            pe.wait_ge(s_d, r)
                        v0 = max(c - 1, 0) * P + gr * DH
                        pe.matmul(misc[rows, :], vwin[0:n, v0:v0 + DH], pT[0:n, :], start=True, stop=True).then_inc(s_pv, 1)

            for t in range(len(IN0)):
                def beside(pc):
                    hgrn(PIECES * t + pc)
                    layernorm(PIECES * t + pc)
                dense(t, ready=in_ready(0) if t == 0 else None, after=x_squares(0) if t == 0 else None, beside=beside)

            def mid_ready(base, blk=0, per=0):
                return lambda k: wait(pe, s_mid, base + k // 2 + 1, blk, per) if k % 2 == 0 else None

            def mid_ready0(k):
                if MID_CONV <= k < MID_CONV + A_TILES:
                    if (k - MID_CONV) % 4 == 0:
                        pe.wait_ge(s_swish, (k - MID_CONV) // 4 + 1)
                elif k % 2 == 0:
                    pe.wait_ge(s_mid, M_OUT0 + (k if k < MID_CONV else k - A_TILES) // 2 + 1)

            def mid_ready1(k):
                if k == 0:
                    pe.wait_ge(s_dlo, 1)
                elif k >= MID_SHORT:
                    pe.wait_ge(s_mid, M_OUT1 + (k - MID_SHORT) // 2 + 1)

            def out_projection(start, ready, n):
                for t in range(OUT_TASKS):
                    dense(start + t, moving=(mid_hi, mid_lo), ready=ready if t == 0 else None)
                norm_sum(n)

            def ffn(start, base, phase, n):
                dense(start, ready=in_ready(phase), after=x_squares(phase))
                for t in range(1, BLOCK):
                    dense(start + t)
                for t in range(BLOCK):
                    dense(start + BLOCK + t, moving=(mid_hi, mid_lo), ready=mid_ready(base) if t == 0 else None)
                with pe.Fori(1, FF_BLOCKS) as blk:
                    for t in range(BLOCK):
                        dense(start + t, blk, 2 * BLOCK)
                    for t in range(BLOCK):
                        dense(start + BLOCK + t, blk, 2 * BLOCK, moving=(mid_hi, mid_lo),
                              ready=mid_ready(base, blk, BLOCK) if t == 0 else None)
                norm_sum(n)

            out_projection(START_OUT0, mid_ready0, 1)
            ffn(START_FF0, M_FF0, 1, 2)

            for t in range(len(IN1)):
                def beside(pc):
                    if PIECES * t + pc == PIECES + 1:
                        pe.wait_ge(s_taken, START_IN1 + 1)
                        for c in range(1, 4):
                            ins = pe.transpose(misc[:, (c - 1) * P:c * P], vT[:, (c - 1) * CHUNK:(c + 1) * CHUNK], ident)
                        ins.then_inc(s_win, 1)
                    attention(PIECES * t + pc)
                dense(START_IN1 + t, ready=in_ready(2) if t == 0 else None, after=x_squares(2) if t == 0 else None,
                      beside=beside)
            out_projection(START_OUT1, mid_ready1, 3)
            ffn(START_FF1, M_FF1, 3, 4)

        @block.scalar
        def _(act):
            ck = Clock(act, s_act)

            def split_piece(i, pc, blk=0, per=0):
                wait(act, s_raw[pc], 16 * (i + 1), blk, 16 * per)
                if i >= 2:
                    wait(act, s_mul, (i - 2) * PIECES + pc + 1, blk, per * PIECES)
                o = ((i % 2) * PIECES + pc) * PW
                act.activation(w_hi[:, o:o + PW], raw[:, pc * PW:(pc + 1) * PW], ACT.Copy).then_inc(s_hi, 1)

            def split(i, blk=0, per=0, between=None, beside=None):
                for pc in range(PIECES):
                    split_piece(i, pc, blk, per)
                    if pc == 1 and between:
                        between()
                    if beside:
                        beside(pc)

            def inverse_rms(n, dst, done):
                act.wait_ge(s_stat, n)
                ck.link(act.activation(dst, stat[:, 0:SEQ], ACT.Ln, scale=1.0 / D, bias=eps))
                act.activation(dst, dst, ACT.Exp, scale=-0.5).then_inc(done, 1)

            def next_input(phase):
                i = (0, START_FF0, START_IN1, START_FF1)[phase]
                for k in range(KT):
                    if phase == 0:
                        if k % KP == 0:
                            split_piece(0, k // KP)
                            act.wait_ge(s_x[k // KP], 16)
                        if k == 0:
                            act.wait_ge(s_vec, 16)
                    else:
                        act.wait_ge(s_xn, (phase - 1) * KT + k + 1)
                    act.activation(tile(in_hi, k), tile(x, k), ACT.Copy,
                                   scale=vcol(V_NORM + 2 * phase * KT + k)).then_inc(s_inh, 1)
                    act.activation(tile(y, k), tile(x, k), ACT.Square).then_inc(s_xsq, 1)
                    for pc in pieces_after(phase, k):
                        split_piece(i + 1, pc)

            def hidden(i, t, blk=0, per=0):
                wait(act, s_taken, i + 1, blk, per)
                ck.link(act.activation(g[:, :], u[:, :], ACT.Square))
                act.activation(tile(mid_hi, MT * t, MT), g[:, :], ACT.Copy).then_inc(s_g, 1)

            def squares(i, t):
                act.wait_ge(s_taken, i + 1)
                act.activation(g[:, :], tile(y, MT * t, MT), ACT.Square).then_inc(s_g, 1)

            def hgrn(tick):
                for j in range(HEADS // 2):
                    if tick == after_task("i", j, IN0) + 2:
                        act.wait_ge(s_vt, j + 1)
                        for m in range(MT):
                            h0 = (2 * j + m) * P
                            ins = act.activation(v3(vtok, HEADS * P)[:, :, h0:h0 + P], v3(stat[:, m * 2 * P:(m + 1) * 2 * P], P),
                                                 ACT.Copy)
                        ins.then_inc(s_vcopy, 1)
                for n in range(HEADS):
                    stage = tick - HEAD_TICK[n]
                    b = tile(bb, n)
                    if stage in (1, 2):
                        act.wait_ge(s_dist, 5 * n + (2 if stage == 1 else 5))
                        some = mm_all[:, SEQ:3 * SEQ] if stage == 1 else mm_all[:, 3 * SEQ:6 * SEQ]
                        ck.link(act.activation(some, some, ACT.Abs))
                        act.activation(some, some, ACT.Exp, scale=-1.0).then_inc(s_dec, 1)
                    if stage == 3:
                        act.activation(v3(mm[6], 2 * CHUNK)[:, :, CHUNK:], v3(b, 2 * CHUNK)[:, :, CHUNK:], ACT.Exp)
                        for dst, c, scale, shift in (
                                (mm[6], 0, -1.0, b[:, CHUNK - 1:CHUNK]), (mm[6], 2, -1.0, b[:, 3 * CHUNK - 1:3 * CHUNK]),
                                (mx_cross, 0, -1.0, tail2[:, n:n + 1]), (mx_cross, 1, -1.0, b[:, 2 * CHUNK - 1:2 * CHUNK]),
                                (mx_cross, 2, 1.0, None), (mx_cross, 3, 1.0, b[:, 3 * CHUNK - 1:3 * CHUNK])):
                            part = slice(c * CHUNK, (c + 1) * CHUNK)
                            if shift is None:
                                ins = act.activation(dst[:, part], b[:, part], ACT.Exp)
                            else:
                                ins = act.activation(dst[:, part], b[:, part], ACT.Exp, scale=scale, bias=shift)
                        ins.then_inc(s_dec, 1)
                    if stage == 8:
                        act.wait_ge(s_lv, n + 1)
                        act.activation(pairs[:, 2 * P:3 * P], misc[:, 2 * P:3 * P], ACT.Copy)
                    if stage == 10:
                        act.wait_ge(s_msum, n + 1)
                        for b in range(P // SUB):
                            rows, after = slice(b * SUB, (b + 1) * SUB), (b + 1) * SUB
                            if after < P:
                                act.activation(v3(pairs[:, :], P)[rows, 0:2, after:],
                                               v3(levels[:, :], 512)[rows, :, FAR + after:FAR + P], ACT.Copy)
                            ins = act.activation(v3(pairs[:, 0:2 * P], P)[rows, :, rows], v3(msum, SUB)[rows, :, :], ACT.Copy)
                        ins.then_inc(s_pairs, 1)
                    if stage == 11:
                        act.wait_ge(s_o, n + 1)
                        ck.link(act.activation(tile(qq, n), misc[:, 0:SEQ], ACT.Copy))
                        act.activation(sqsum[:, :], tile(qq, n), ACT.Square).then_inc(s_osq, 1)
                    if stage == 12:
                        act.wait_ge(s_on, n + 1)
                        ck.link(act.activation(sqsum[:, :], misc[:, 2 * P:4 * P], ACT.Ln, scale=1.0 / P, bias=eps))
                        act.activation(sqsum[:, :], sqsum[:, :], ACT.Exp, scale=-0.5).then_inc(s_or, 1)

            def layernorm(tick):
                stage = tick - NORM_TICK
                if stage in (2, 3):
                    h = stage - 2
                    act.wait_ge(s_cent, h + 1)
                    if h:
                        act.wait_ge(s_lnsq, h)
                    act.activation(lnsq, tile(conv, 4 * h, 4), ACT.Square).then_inc(s_csq, 1)
                if stage == 4:
                    act.wait_ge(s_lnsq, 2)
                    ck.link(act.activation(acc2[:, :], stat[:, SEQ:2 * SEQ], ACT.Ln, scale=1.0 / (A_TILES * P), bias=eps))
                    act.activation(acc2[:, :], acc2[:, :], ACT.Exp, scale=-0.5).then_inc(s_lnr, 1)
                if stage in (6, 7):
                    h = stage - 6
                    act.wait_ge(s_lnn, h + 1)
                    for j in range(4 * h, 4 * h + 4):
                        ck.mark(act.activation(tile(conv, j), tile(conv, j), ACT.Identity, scale=vcol(V_LNW + j), bias=vcol(V_LNB + j)))
                    ck.settle()
                    if h:
                        act.wait_ge(s_lns, h)
                    act.activation(lnsq, tile(conv, 4 * h, 4), ACT.Sigmoid).then_inc(s_lna, 1)
                if stage in (7, 8):
                    h = stage - 7
                    act.wait_ge(s_lns, h + 1)
                    act.activation(tile(mid_hi, MID_CONV + 4 * h, 4), tile(conv, 4 * h, 4), ACT.Copy).then_inc(s_lnh, 1)

            def attention(tick):
                for r, t0 in enumerate(ATT_TICK):
                    stage = tick - t0
                    c, gr = r // GROUPS, r % GROUPS
                    n = CHUNK if c == 0 else WIN
                    rows = slice(gr * DH, (gr + 1) * DH)
                    if stage == 2:
                        act.wait_ge(s_sm, r + 1)
                        act.activation(esink, esink, ACT.Exp)
                        s4 = v3(sc, P)[:, :, 0:n]
                        act.activation(s4, s4, ACT.Exp).then_inc(s_ex, 1)
                    if stage == 5:
                        act.wait_ge(s_pt, r + 1)
                        act.activation(pT[0:n, :], lev[1][0:n, :], ACT.Copy).then_inc(s_ptc, 1)
                    if stage == 7:
                        act.wait_ge(s_pv, r + 1)
                        act.activation(v3(dT, SEQ)[rows, :, c * CHUNK:(c + 1) * CHUNK], v3(misc[rows, :], CHUNK),
                                       ACT.Copy).then_inc(s_d, 1)
                if tick == ATT_END:
                    act.wait_ge(s_d, len(ATT_TICK))
                    act.activation(tile(mid_hi, 0, MID_SHORT), dT, ACT.Copy).then_inc(s_dhi, 1)

            act.wait_ge(s_eps, 1)
            ck.link(act.activation(small[:, 1:2], eps, ACT.Copy))
            next_input(0)

            act.wait_ge(s_lbx, 1)
            act.activation(small[:, 32:48], small[:, 32:48], ACT.Exp).then_inc(s_lbe, 1)
            def gated_high(j):
                act.wait_ge(s_gate, j + 1)
                act.activation(tile(mid_hi, mid_head(2 * j), 2), g[:, :], ACT.Copy).then_inc(s_gate_hi, 1)

            def sigmoids(t):
                kind, j = IN0[t]
                if kind not in "afg":
                    return
                act.wait_ge(s_taken, t + 1)
                if kind == "a":
                    act.activation(g[:, 0:SEQ], u[:, SEQ:2 * SEQ], ACT.Sigmoid).then_inc(s_g, 1)
                    return
                if kind == "g" and j:
                    act.wait_ge(s_mid, j)
                act.activation(g[:, :], u[:, :], ACT.Sigmoid).then_inc(s_g, 1)
                if kind == "f":
                    act.wait_ge(s_bound, 1)
                    act.wait_ge(s_g, G0[t])
                    for m in range(MT):
                        n = 2 * j + m
                        act.activation(tile(kk, n), tile(g, m), ACT.Identity, scale=nomlb[:, n:n + 1], bias=omlb[:, n:n + 1])
                    for m in range(MT):
                        n = 2 * j + m
                        ins = act.activation(tile(bb, n), tile(g, m), ACT.Ln, scale=omlb[:, n:n + 1], bias=lb[:, n:n + 1])
                    ins.then_inc(s_lnf, 1)
                    act.wait_ge(s_lnf, j + 1)

            inverse_rms(1, rpre[:, :], s_rpre)
            for pc in range(LEAD):
                split_piece(2, pc)
            for t in range(1, len(IN0)):
                for pc in range(PIECES):
                    ahead = PIECES * (t + 1) + pc + LEAD
                    if ahead < PIECES * (len(IN0) + 1):
                        split_piece(ahead // PIECES, ahead % PIECES)
                    if pc == 1:
                        sigmoids(t - 1)
                    if pc == 3 and IN0[t - 1][0] == "g":
                        gated_high(IN0[t - 1][1])
                    hgrn(PIECES * t + pc)
                    layernorm(PIECES * t + pc)

            def out_projection(start, left=None):
                for t in range(OUT_TASKS):
                    split(start + t + 1, beside=left if t == 0 else None)
                    squares(start + t, t)

            def ffn(start, n):
                per = 2 * BLOCK
                for t in range(BLOCK):
                    if t == 0:
                        inverse_rms(n, rpre[:, :], s_rpre)
                    else:
                        split(start + t + 1)
                    hidden(start + t, t)
                for t in range(BLOCK):
                    split(start + BLOCK + t + 1)
                n0 = ck.n
                with act.Fori(1, FF_BLOCKS - 1) as blk:
                    ck.rt = (blk - 1) * BLOCK
                    for t in range(BLOCK):
                        split(start + t + 1, blk, per)
                        hidden(start + t, t, blk, per)
                    for t in range(BLOCK):
                        split(start + BLOCK + t + 1, blk, per)
                assert ck.n == n0 + BLOCK
                ck.rt, ck.n = 0, n0 + BLOCK * (FF_BLOCKS - 2)
                s2 = start + per * (FF_BLOCKS - 1)
                for t in range(BLOCK):
                    split(s2 + t + 1)
                    hidden(s2 + t, t)
                for t in range(BLOCK):
                    if s2 + BLOCK + t + 1 < TASKS:
                        split(s2 + BLOCK + t + 1)
                    squares(s2 + BLOCK + t, t)

            def last_gate(pc):
                if pc == 1:
                    sigmoids(len(IN0) - 1)
                if pc == 2:
                    gated_high(HEADS // 2 - 1)

            out_projection(START_OUT0, last_gate)
            inverse_rms(2, rpost[:, :], s_rpost)
            next_input(1)
            ffn(START_FF0, 3)
            inverse_rms(4, rpost[:, :], s_rpost)
            next_input(2)

            def c_high(t):
                kind, j = IN1[t]
                if kind == "c" and j % 3:
                    n = 2 * (j // 3) + (j % 3 - 1)
                    act.wait_ge(s_c, n + 1)
                    act.activation(tile(mid_hi, MID_SHORT + n), cacc, ACT.Copy).then_inc(s_chi, 1)

            inverse_rms(5, rpre[:, :], s_rpre)
            for pc in range(LEAD):
                split_piece(START_IN1 + 2, pc)
            for t in range(1, len(IN1)):
                for pc in range(PIECES):
                    ahead = PIECES * (t + 1) + pc + LEAD
                    if ahead < PIECES * (len(IN1) + 1):
                        split_piece(START_IN1 + ahead // PIECES, ahead % PIECES)
                    if pc == 2:
                        c_high(t - 1)
                    attention(PIECES * t + pc)

            def last_c(pc):
                if pc == 1:
                    c_high(len(IN1) - 1)

            out_projection(START_OUT1, last_c)
            inverse_rms(6, rpost[:, :], s_rpost)
            next_input(3)
            ffn(START_FF1, 7)
            inverse_rms(8, rpost[:, :], s_rpost)

        @block.vector
        def _(dve):
            ck = Clock(dve, s_dve)

            def split_piece(i, pc, blk=0, per=0):
                wait(dve, s_hi, i * PIECES + pc + 1, blk, per * PIECES)
                o = ((i % 2) * PIECES + pc) * PW
                dve.tensor_tensor(w_lo[:, o:o + PW], raw[:, pc * PW:(pc + 1) * PW], w_hi[:, o:o + PW],
                                  ALU.subtract).then_inc(s_lo, 1)

            def split(i, blk=0, per=0, between=None, beside=None):
                for pc in range(PIECES):
                    split_piece(i, pc, blk, per)
                    if pc == 1 and between:
                        between()
                    if beside:
                        beside(pc)

            def result(i, blk=0, per=0):
                wait(dve, s_mul, (i + 1) * PIECES, blk, per * PIECES)
                return v3(dense_bank[i % 4][:, :], SEQ)

            def scaled(dst, i):
                return dve.tensor_tensor(v3(dst, SEQ), result(i), per_token(rpre[:, :], MT), ALU.mult)

            def next_input(phase, alone=T_DVE):
                i = (0, START_FF0, START_IN1, START_FF1, 0)[phase]
                if phase == 0:
                    dve.wait_ge(s_vec, 16)
                else:
                    dve.wait_ge(s_rpost, phase)

                def updated(k):
                    if phase == 0:
                        if k % KP == 0:
                            split_piece(0, k // KP)
                        return
                    if k < alone:
                        if k == 0:
                            ck.mark(dve.tensor_tensor(tile(y, k), tile(y, k), rpost[:, :], ALU.mult))
                        if k + 1 < alone:
                            ck.mark(dve.tensor_tensor(tile(y, k + 1), tile(y, k + 1), rpost[:, :], ALU.mult))
                        ck.settle(1 if k + 1 < alone else 0)
                    else:
                        dve.wait_ge(s_yr, (phase - 1) * (KT - T_DVE) + k - alone + 1)
                    dve.scalar_tensor_tensor(out=tile(x, k), in0=tile(y, k), scalar=vcol(V_NORM + (2 * phase - 1) * KT + k),
                                             in1=tile(x, k), op0=ALU.mult, op1=ALU.add).then_inc(s_xn, 1)

                updated(0)
                for k in range(KT):
                    if k + 1 < KT:
                        updated(k + 1)
                    if phase == 4:
                        continue
                    dve.wait_ge(s_inh, phase * KT + k + 1)
                    dve.scalar_tensor_tensor(out=tile(in_lo, k), in0=tile(x, k), scalar=vcol(V_NORM + 2 * phase * KT + k),
                                             in1=tile(in_hi, k), op0=ALU.mult, op1=ALU.subtract).then_inc(s_inl, 1)
                    for pc in pieces_after(phase, k):
                        split_piece(i + 1, pc)

            dve.memset(small[:, :], EPS).then_inc(s_eps, 1)
            ck.mark(dve.memset(hpad, 0.0))
            ck.link(dve.memset(pairs[:, :], 0.0))
            next_input(0)
            l0, l1 = vec[:, V_LB:V_LB + HEADS], vec[:, V_LB + HEADS:V_LB + 2 * HEADS]
            e0, e1, top = small[:, 32:40], small[:, 40:48], small[:, 48:56]
            ck.link(dve.tensor_tensor(top, l0, l1, ALU.max))
            ck.link(dve.tensor_tensor(e0, l0, top, ALU.subtract))
            dve.tensor_tensor(e1, l1, top, ALU.subtract).then_inc(s_lbx, 1)
            dve.wait_ge(s_lbe, 1)
            ck.link(dve.tensor_tensor(top, e0, e1, ALU.add))
            ck.link(dve.reciprocal(top, top))
            ck.link(dve.tensor_tensor(lb, e0, top, ALU.mult))
            ck.link(dve.tensor_scalar(omlb, lb, -1.0, 1.0, ALU.mult, ALU.add))
            dve.tensor_scalar(nomlb, lb, 1.0, -1.0, ALU.mult, ALU.add).then_inc(s_bound, 1)

            def late0(t):
                if t < 0 or IN0[t][0] not in "afg":
                    return
                kind, j = IN0[t]
                dve.wait_ge(s_g, G0[t])
                if kind == "a":
                    o = (j % HBUF) * HP + A_CONV - 1
                    ck.link(dve.tensor_tensor(hpad[:, o:o + SEQ], u[:, 0:SEQ], g[:, 0:SEQ], ALU.mult))
                elif kind == "g":
                    ck.link(dve.tensor_tensor(g[:, :], u[:, :], g[:, :], ALU.mult))
                    dve.tensor_tensor(g[:, :], g[:, :], tile(qq, 2 * j, 2), ALU.mult).then_inc(s_gate, 1)

            def gated_low(t):
                if t > 0 and IN0[t][0] == "g":
                    j = IN0[t][1]
                    dve.wait_ge(s_gate_hi, j + 1)
                    dve.tensor_tensor(tile(mid_lo, mid_head(2 * j), 2), g[:, :], tile(mid_hi, mid_head(2 * j), 2), ALU.subtract).then_inc(s_mid, 1)

            def hgrn(tick):
                for j in range(HEADS // 2):
                    if tick == SCAN_TICK[j]:
                        dve.wait_ge(s_lnf, j + 1)
                        for n in (2 * j, 2 * j + 1):
                            ck.mark(dve.tensor_tensor_scan(tile(bb, n), con[:, C_RESET:C_RESET + SEQ], tile(bb, n), 0.0,
                                                           ALU.mult, ALU.add))
                        ck.settle()
                        b3 = v3(tile(bb, 2 * j, 2), SEQ)
                        ck.link(dve.tensor_tensor(tail2[:, 2 * j:2 * j + 2].unsqueeze(2), b3[:, :, CHUNK - 1:CHUNK],
                                                  b3[:, :, 2 * CHUNK - 1:2 * CHUNK], ALU.add))
                for n in range(HEADS):
                    stage = tick - HEAD_TICK[n]
                    b, k, q = tile(bb, n), tile(kk, n), tile(qq, n)
                    w1 = LEVELS * SUB

                    def decayed(m, half):
                        m3, k3, q3 = (v3(z, 2 * half) for z in (m, k, q))
                        ck.mark(dve.tensor_tensor(m3[:, :, 0:half], m3[:, :, 0:half], k3[:, :, 0:half], ALU.mult))
                        return dve.tensor_tensor(m3[:, :, half:], m3[:, :, half:], q3[:, :, half:], ALU.mult)

                    if stage in (0, 1):
                        if n and stage == 0:
                            dve.wait_ge(s_lv, n)
                        for l, half in list(enumerate(HALVES[1:]))[(1, 3)[stage]:(3, 6)[stage]]:
                            m3, b3 = v3(mm[l], 2 * half), v3(b, 2 * half)
                            ref = b3[:, :, half - 1:half].to_broadcast([P, SEQ // (2 * half), 2 * half])
                            ins = dve.tensor_tensor(m3, b3, ref, ALU.subtract)
                            ins.then_inc(s_dist, 1)
                    if stage in (3, 4):
                        dve.wait_ge(s_dec, 3 * n + stage - 2)
                        if stage == 3:
                            ck.mark(dve.scalar_tensor_tensor(out=mm[0], in0=k, scalar=1.0, in1=q, op0=ALU.subtract, op1=ALU.mult))
                        for l, half in list(enumerate(HALVES[1:]))[(1, 3)[stage - 3]:(3, 6)[stage - 3]]:
                            ck.mark(decayed(mm[l], half))
                    if stage == 5:
                        dve.wait_ge(s_dec, 3 * n + 3)
                        ck.mark(decayed(mm[6], CHUNK))
                        decayed(mx_cross, P).then_inc(s_kq, 1)
                    if stage == 8:
                        dve.wait_ge(s_lv, n + 1)
                        mask = con[:, C_MASK:C_MASK + w1].unsqueeze(1).to_broadcast([P, 2, w1])
                        ck.link(dve.tensor_tensor(v3(masked, w1), v3(levels[:, :], 512)[:, :, 0:w1], mask, ALU.mult))
                    if stage == 9:
                        dve.tensor_reduce(v3(msum, SUB), masked.rearrange("p (a l t) -> p a t l", a=2, l=LEVELS), AX_X,
                                          ALU.add).then_inc(s_msum, 1)
                    if stage == 13:
                        dve.wait_ge(s_or, n + 1)
                        ck.link(dve.scalar_tensor_tensor(out=q, in0=q, scalar=vcol(V_BN), in1=sqsum[:, :], op0=ALU.mult, op1=ALU.mult))

            def layernorm(tick):
                stage = tick - NORM_TICK

                def half(h):
                    return v3(tile(conv, 4 * h, 4), SEQ)
                if stage == 1:
                    dve.wait_ge(s_lnsum, 1)
                    ck.link(dve.tensor_scalar(acc2[:, :], stat[:, 0:SEQ], 1.0 / (A_TILES * P), None, ALU.mult))
                    for h in range(2):
                        dve.tensor_tensor(half(h), half(h), per_token(acc2[:, :], 4), ALU.subtract).then_inc(s_cent, 1)
                if stage == 5:
                    dve.wait_ge(s_lnr, 1)
                    for h in range(2):
                        dve.tensor_tensor(half(h), half(h), per_token(acc2[:, :], 4), ALU.mult).then_inc(s_lnn, 1)
                if stage in (6, 7):
                    h = stage - 6
                    dve.wait_ge(s_lna, h + 1)
                    dve.tensor_tensor(tile(conv, 4 * h, 4), tile(conv, 4 * h, 4), lnsq, ALU.mult).then_inc(s_lns, 1)
                if stage in (8, 9):
                    h = stage - 8
                    dve.wait_ge(s_lnh, h + 1)
                    dve.tensor_tensor(tile(mid_lo, MID_CONV + 4 * h, 4), tile(conv, 4 * h, 4), tile(mid_hi, MID_CONV + 4 * h, 4),
                                      ALU.subtract).then_inc(s_swish, 1)

            def attention(tick):
                for r, t0 in enumerate(ATT_TICK):
                    stage = tick - t0
                    c, gr = r // GROUPS, r % GROUPS
                    n = CHUNK if c == 0 else WIN
                    s4, b4 = v3(sc, P)[:, :, 0:n], v3(wk[:, gr * 512:(gr + 1) * 512], P)[:, :, WIN - n:]
                    sink = vec[:, V_SINK + 4 * gr:V_SINK + 4 * gr + 4]

                    def per_row(a):
                        return a.unsqueeze(2).to_broadcast([P, 4, n])

                    if stage == 1:
                        if r == 0:
                            dve.wait_ge(s_bias, 16)
                        dve.wait_ge(s_sc, r + 1)
                        ck.link(dve.tensor_tensor(s4, v3(lev[0], P)[:, :, 0:n], b4, ALU.add))
                        ck.link(dve.tensor_reduce(mx, s4, AX_X, ALU.max))
                        ck.link(dve.tensor_tensor(mx, mx, sink, ALU.max))
                        ck.mark(dve.tensor_tensor(esink, sink, mx, ALU.subtract))
                        dve.tensor_tensor(s4, s4, per_row(mx), ALU.subtract).then_inc(s_sm, 1)
                    if stage == 3:
                        dve.wait_ge(s_ex, r + 1)
                        ck.link(dve.tensor_reduce(den, s4, AX_X, ALU.add))
                        ck.link(dve.tensor_tensor(den, den, esink, ALU.add))
                        ck.link(dve.reciprocal(rden, den))
                        dve.tensor_tensor(s4, s4, per_row(rden), ALU.mult).then_inc(s_p, 1)
                if tick == ATT_END + 1:
                    dve.wait_ge(s_dhi, 1)
                    dve.tensor_tensor(tile(mid_lo, 0, MID_SHORT), dT, tile(mid_hi, 0, MID_SHORT), ALU.subtract).then_inc(s_dlo, 1)

            def convolve(tick):
                for j, q in CONV_TAPS.get(tick, ()):
                    h = hpad[:, (j % HBUF) * HP:(j % HBUF + 1) * HP]
                    a = tile(conv, j)
                    wq = vcol(V_DW + j * A_CONV + q)
                    dst = a if q % 2 == 0 else acc2[:, :]
                    if q == 0:
                        ck.mark(dve.tensor_scalar(dst, h[:, 0:SEQ], wq, vcol(V_DWB + j), ALU.mult, ALU.add))
                    elif q == 1:
                        if j:
                            dve.wait_ge(s_conv, j)
                        ck.mark(dve.tensor_scalar(dst, h[:, 1:1 + SEQ], wq, None, ALU.mult))
                    else:
                        ck.settle(1)
                        ck.mark(dve.scalar_tensor_tensor(out=dst, in0=h[:, q:q + SEQ], scalar=wq, in1=dst,
                                                         op0=ALU.mult, op1=ALU.add))
                    if q == A_CONV - 1:
                        ck.settle()
                        dve.tensor_tensor(a, a, acc2[:, :], ALU.add).then_inc(s_conv, 1)

            def take0(t):
                kind, j = IN0[t]
                if t and IN0[t - 1][0] == "i":
                    dve.wait_ge(s_vt, IN0[t - 1][1] + 1)
                dst = tile(qq, 2 * j, 2) if kind == "q" else u[:, :]
                scaled(dst, t).then_inc(s_taken, 1)
                dve.wait_ge(s_taken, t + 1)

            dve.wait_ge(s_rpre, 1)
            for t in range(1, len(IN0)):
                for pc in range(PIECES):
                    tick = PIECES * t + pc
                    split_piece(t + 1, pc)
                    if pc == 0:
                        gated_low(t - 2)
                        take0(t - 1)
                    if pc == 2:
                        late0(t - 1)
                    hgrn(tick)
                    convolve(tick)
                    layernorm(tick)

            def last_gate(pc):
                if pc == 0:
                    gated_low(len(IN0) - 2)
                    take0(len(IN0) - 1)
                if pc == 2:
                    late0(len(IN0) - 1)
                    gated_low(len(IN0) - 1)

            def add_squares(ui):
                dve.wait_ge(s_g, ui + 1)
                ck.link(dve.tensor_tensor(sqsum[:, :], sqsum[:, :], g[:, 0:SEQ], ALU.add))
                ins = dve.tensor_tensor(sqsum[:, :], sqsum[:, :], g[:, SEQ:2 * SEQ], ALU.add)
                return ins

            def finish_squares(ui):
                add_squares(ui).then_inc(s_sum, 1)

            def out_projection(start, gi, left=None):
                for t in range(OUT_TASKS):
                    split(start + t + 1, between=(lambda: ck.link(add_squares(gi + t - 1))) if t else None,
                          beside=left if t == 0 else None)
                    if t == 0:
                        ck.link(dve.memset(sqsum[:, :], 0.0))
                    dve.tensor_copy(v3(tile(y, MT * t, MT), SEQ), result(start + t)).then_inc(s_taken, 1)
                finish_squares(gi + OUT_TASKS - 1)

            def up(i, blk=0, per=0):
                dve.scalar_tensor_tensor(out=v3(u[:, :], SEQ), in0=result(i, blk, per), scalar=0.0,
                                         in1=per_token(rpre[:, :], MT), op0=ALU.max, op1=ALU.mult).then_inc(s_taken, 1)

            def low_hidden(gi, t, blk=0, per=0):
                wait(dve, s_g, gi + 1, blk, per)
                dve.tensor_tensor(tile(mid_lo, MT * t, MT), g[:, :], tile(mid_hi, MT * t, MT), ALU.subtract).then_inc(s_mid, 1)

            def down(i, t, first=False, blk=0, per=0):
                r = result(i, blk, per)
                dst = v3(tile(y, MT * t, MT), SEQ)
                ins = dve.tensor_copy(dst, r) if first else dve.tensor_tensor(dst, r, dst, ALU.add)
                ins.then_inc(s_taken, 1)

            def ffn(start, gi, n):
                per = 2 * BLOCK

                def ups(s0, g0, blk=0):
                    p, q = (per, BLOCK) if not isinstance(blk, int) else (0, 0)
                    for t in range(BLOCK):
                        if s0 == start and t == 0 and p == 0:
                            dve.wait_ge(s_rpre, n)
                        else:
                            split(s0 + t + 1, blk, p, between=(lambda: low_hidden(g0 + t - 1, t - 1, blk, q)) if t else None)
                        up(s0 + t, blk, p)
                    return lambda: low_hidden(g0 + BLOCK - 1, BLOCK - 1, blk, q)

                left = ups(start, gi)
                for t in range(BLOCK):
                    split(start + BLOCK + t + 1, between=left if t == 0 else None)
                    down(start + BLOCK + t, t, first=True)
                with dve.Fori(1, FF_BLOCKS - 1) as blk:
                    left = ups(start, gi, blk)
                    for t in range(BLOCK):
                        split(start + BLOCK + t + 1, blk, per, between=left if t == 0 else None)
                        down(start + BLOCK + t, t, blk=blk, per=per)
                s2, g2 = start + per * (FF_BLOCKS - 1), gi + BLOCK * (FF_BLOCKS - 1)
                left = ups(s2, g2)
                ck.link(dve.memset(sqsum[:, :], 0.0))
                for t in range(BLOCK):
                    i = s2 + BLOCK + t
                    between = left if t == 0 else (lambda: ck.link(add_squares(g2 + BLOCK + t - 1)))
                    if i + 1 < TASKS:
                        split(i + 1, between=between)
                    else:
                        between()
                    down(i, t)
                finish_squares(g2 + 2 * BLOCK - 1)

            out_projection(START_OUT0, G_OUT0, last_gate)
            dve.wait_ge(s_back, 16)
            next_input(1)
            ffn(START_FF0, G_FF0, 2)
            next_input(2)

            def c_low(t):
                kind, j = IN1[t]
                if kind == "c" and j % 3:
                    n = 2 * (j // 3) + (j % 3 - 1)
                    dve.wait_ge(s_chi, n + 1)
                    ins = dve.tensor_tensor(tile(mid_lo, MID_SHORT + n), cacc, tile(mid_hi, MID_SHORT + n), ALU.subtract)
                    if n % 2:
                        ins.then_inc(s_mid, 1)
                    else:
                        ck.link(ins)

            def take1(t):
                kind, j = IN1[t]
                i = START_IN1 + t
                if kind == "kv":
                    scaled(x[:, 0:512], i).then_inc(s_taken, 1)
                elif kind == "q":
                    r = result(i)
                    for m in range(MT):
                        dst = v3(qT, C_TILES * CHUNK)[:, :, (2 * j + m) * CHUNK:(2 * j + m + 1) * CHUNK]
                        ins = dve.scalar_tensor_tensor(out=dst, in0=v3(r[:, m, :], CHUNK), scalar=DH ** -0.5,
                                                       in1=v3(rpre[:, :], CHUNK), op0=ALU.mult, op1=ALU.mult)
                    ins.then_inc(s_taken, 1)
                else:
                    scaled(tile(cbuf, 2 * (j % 3), 2), i).then_inc(s_taken, 1)
                if kind == "c" and j % 3:
                    dve.wait_ge(s_taken, i + 1)
                    n = 2 * (j // 3) + (j % 3 - 1)
                    hh, cc, gb = ((0, 1, 2), (3, 4, 5))[j % 3 - 1]
                    ck.link(dve.tensor_tensor(cpad[:, 2:2 + SEQ], tile(cbuf, hh), tile(cbuf, cc), ALU.mult))
                    for q in range(C_CONV):
                        wq = vcol(V_CC + n * C_CONV + q)
                        if q == 0:
                            ck.link(dve.tensor_scalar(cacc, cpad[:, 0:SEQ], wq, None, ALU.mult))
                        else:
                            ck.link(dve.scalar_tensor_tensor(out=cacc, in0=cpad[:, q:q + SEQ], scalar=wq, in1=cacc,
                                                             op0=ALU.mult, op1=ALU.add))
                    dve.tensor_tensor(cacc, cacc, tile(cbuf, gb), ALU.mult).then_inc(s_c, 1)

            dve.wait_ge(s_rpre, 3)
            dve.wait_ge(s_spill, 16)
            for t in range(1, len(IN1)):
                for pc in range(PIECES):
                    tick = PIECES * t + pc
                    split_piece(START_IN1 + t + 1, pc)
                    if pc == 0:
                        take1(t - 1)
                    if pc == 3:
                        c_low(t - 1)
                    if tick == PIECES + 2:
                        dve.wait_ge(s_win, 1)
                        ck.mark(dve.tensor_copy(vwin, misc[:, 0:3 * P]))
                        ck.link(dve.memset(cpad, 0.0))
                    attention(tick)

            def last_c(pc):
                if pc == 0:
                    take1(len(IN1) - 1)
                if pc == 2:
                    c_low(len(IN1) - 1)

            out_projection(START_OUT1, G_OUT1, last_c)
            dve.wait_ge(s_back, 32)
            next_input(3)
            ffn(START_FF1, G_FF1, 4)
            next_input(4, T_DVE_LAST)


def _tiles(v):
    v = np.asarray(v)
    return v.reshape(v.shape[:-1] + (v.shape[-1] // P, P))


def _columns():
    r = np.arange(P)
    aw, hw = A_TILES * P, HEADS * P
    base = {"f": 2 * aw + hw, "q": 2 * aw, "i": 2 * aw + 2 * hw, "g": 2 * aw + 3 * hw}
    in0 = []
    for kind, j in IN0:
        if kind == "a":
            in0.append(np.concatenate([j * P + r, aw + j * P + r]))
        else:
            in0.append(base[kind] + 2 * j * P + np.arange(2 * P))
    cw = C_TILES * P
    qb, kb = 3 * cw, 3 * cw + Q_HEADS * DH
    in1 = []
    d = np.arange(DH)
    order = []
    for j in range(C_TILES // 2):
        order += [(0, 2 * j), (2, 2 * j), (1, 2 * j), (0, 2 * j + 1), (2, 2 * j + 1), (1, 2 * j + 1)]
    for kind, j in IN1:
        if kind == "kv":
            in1.append(kb + np.arange(2 * P))
        elif kind == "q":
            in1.append(np.concatenate([qb + h * DH + d for n in (2 * j, 2 * j + 1) for h in (n, Q_HEADS // 2 + n)]))
        else:
            in1.append(np.concatenate([part * cw + n * P + r for part, n in order[2 * j:2 * j + 2]]))
    return np.concatenate(in0), np.concatenate(in1)


def _head_rows():
    d = np.arange(DH)
    return np.concatenate([h * DH + d for n in range(Q_HEADS // 2) for h in (n, Q_HEADS // 2 + n)])


def _stream(parts):
    out = np.empty((TASKS, P, KT, COLS), np.float32)
    at = 0
    for m in parts:
        n = m.shape[1] // COLS
        out[at:at + n] = m.reshape(KT, P, n, COLS).transpose(2, 1, 0, 3)
        at += n
    assert at == TASKS
    return out.reshape(TASKS, P, KT * COLS)


def _constants():
    con = np.zeros((P, C_N), np.float32)
    con[:, C_ID:C_ID + P] = np.eye(P)
    con[:, C_ONE:C_ONE + P] = 1
    s, t = np.arange(P)[:, None] % SUB, np.arange(SUB)[None, :]
    for l, half in enumerate(HALVES[:LEVELS]):
        if half == 0:
            m = s == t
        else:
            m = (s // (2 * half) == t // (2 * half)) & (s % (2 * half) < half) & (t % (2 * half) >= half)
        con[:, C_MASK + l * SUB:C_MASK + (l + 1) * SUB] = -1.0 * m if half == 1 else m
    con[:, C_RESET:C_RESET + SEQ] = (np.arange(SEQ) % CHUNK != 0)
    slopes = (2.0 ** (-8.0 * np.arange(1, Q_HEADS + 1, dtype=np.float32) / Q_HEADS)).astype(np.float32)
    dist = np.abs(np.arange(CHUNK)[:, None] + CHUNK - np.arange(WIN)[None, :]).astype(np.float32)
    bias = np.zeros((2, CHUNK, GROUPS, 4, WIN), np.float32)
    for gr in range(GROUPS):
        for jp in range(4):
            for e in range(2):
                bias[e, :, gr, jp, :] = -slopes[8 * gr + 2 * jp + e] * dist
    return con, bias.reshape(P, GROUPS * 4 * WIN)


def kernel(x, w_in_even, w_out_even, a_dw_w, a_dw_b, a_ln_w, a_ln_b, b_lb_logits, b_norm_w, w_in_odd, w_out_odd,
           c_conv_w, d_sinks, norm_pre_mix, norm_post_mix, norm_pre_ffn, norm_post_ffn, w_ffn_up, w_ffn_down):
    import concourse.bacc as bacc
    from concourse.bass_utils import run_bass_kernel_spmd

    cols0, cols1 = _columns()
    aw, hw = A_TILES * P, MID_CONV * P
    rows0 = np.concatenate([aw + np.arange(hw), np.arange(aw), aw + hw + np.arange(D - aw - hw)])
    rows1 = np.concatenate([C_TILES * P + _head_rows(), np.arange(C_TILES * P)])

    def ffn(l):
        up, down = np.asarray(w_ffn_up)[l], np.asarray(w_ffn_down)[l]
        return [m for b in range(FF_BLOCKS) for m in (up[:, b * D:(b + 1) * D], down[b * D:(b + 1) * D])]

    stream = _stream([np.asarray(w_in_even)[0][:, cols0], np.asarray(w_out_even)[0][rows0], *ffn(0),
                      np.asarray(w_in_odd)[0][:, cols1], np.asarray(w_out_odd)[0][rows1], *ffn(1)])
    vec = np.empty((P, V_N), np.float32)
    norms = [np.asarray(v)[l] for l in range(2) for v in (norm_pre_mix, norm_post_mix, norm_pre_ffn, norm_post_ffn)]
    for n, v in enumerate(norms):
        vec[:, V_NORM + n * KT:V_NORM + (n + 1) * KT] = _tiles(v).T
    vec[:, V_DW:V_DWB] = _tiles(a_dw_w[0]).transpose(2, 1, 0).reshape(P, A_TILES * A_CONV)
    vec[:, V_DWB:V_LNW] = _tiles(a_dw_b[0]).T
    vec[:, V_LNW:V_LNB] = _tiles(a_ln_w[0]).T
    vec[:, V_LNB:V_LB] = _tiles(a_ln_b[0]).T
    vec[:, V_LB:V_BN] = _tiles(b_lb_logits).transpose(2, 0, 1).reshape(P, 2 * HEADS)
    vec[:, V_BN] = np.asarray(b_norm_w)[0]
    vec[:, V_CC:V_SINK] = _tiles(c_conv_w[0]).transpose(2, 1, 0).reshape(P, C_TILES * C_CONV)
    sinks = np.asarray(d_sinks)[0].reshape(GROUPS, 4, 2)
    vec[:, V_SINK:] = np.repeat(sinks.transpose(2, 0, 1).reshape(2, 1, 8), CHUNK, axis=1).reshape(P, 8)
    con, bias = _constants()
    xt = np.ascontiguousarray(np.asarray(x)[0].T.reshape(KT, P, SEQ).transpose(1, 0, 2)).reshape(P, KT * SEQ)

    arrays = {"weights": stream, "x_in": xt, "vectors": vec, "constants": con, "alibi": bias}
    nc = bacc.Bacc("TRN2", target_bir_lowering=False, num_devices=1)
    ins = [nc.dram_tensor(k, a.shape, F32, kind="ExternalInput").ap() for k, a in arrays.items()]
    xsave = nc.dram_tensor("x_save", (P, KT * SEQ), F32, kind="Internal").ap()
    out = nc.dram_tensor("out", (P, KT * SEQ), F32, kind="ExternalOutput").ap()
    bass_hybrid_trunk(nc, *ins, xsave, out)
    r = run_bass_kernel_spmd(nc, [arrays], core_ids=[0])
    got = r.results[0]["out"]
    return np.ascontiguousarray(got.reshape(P, KT, SEQ).transpose(2, 1, 0)).reshape(1, SEQ, D)
```
